# Optimizing a Trainium2 kernel written in Bass

```python
import jax, jax.numpy as jnp
from jax import lax
import numpy as np

D_MODEL = 1024
BATCH = 1
SEQ = 512
DEPTH = 1

CTX_LEN = 256
GRID_W = 64
N_MIXERS = 2
EPS = 1e-6
N_MOD = 6
HG_EXPAND = 128
HG_HEADS = D_MODEL // HG_EXPAND
HG_DV = D_MODEL // HG_HEADS
HG_CHUNK = 64
N_HG_PROJ = 5
POOL_WINDOWS = (2, 4, 8, 16)
POOL_GROUPS = len(POOL_WINDOWS)
POOL_GDIM = D_MODEL // POOL_GROUPS
N_EXPERTS = 16
N_EXPERT_GROUPS = 4
EXPERTS_PER_GROUP = N_EXPERTS // N_EXPERT_GROUPS
TOP_K = 2
D_EXPERT = 256


def rms_norm(x, g):
    xf = x.astype(jnp.float32)
    y = xf * lax.rsqrt(jnp.mean(xf * xf, axis=-1, keepdims=True) + EPS)
    return (y * g.astype(jnp.float32)).astype(x.dtype)

def modulate(x, g, shift, scale):
    return rms_norm(x, g) * (1.0 + scale) + shift

def _heads(t):
    b, l, _ = t.shape
    return t.reshape(b, l, HG_HEADS, -1).transpose(0, 2, 1, 3).astype(jnp.float32)

def _rev(t):
    return jnp.flip(t, axis=2)

def _lower_bound(logits, slot):
    p = jax.nn.softmax(logits.astype(jnp.float32), axis=0)
    return jnp.cumsum(p, axis=0)[slot].reshape(HG_HEADS, 1, HG_EXPAND)

def _gate(z, lb):
    log_f = jnp.logaddexp(jnp.log(lb), jnp.log1p(-lb) + jax.nn.log_sigmoid(z))
    k = (1.0 - lb) * jax.nn.sigmoid(-z)
    return log_f, k

def _gla_scan(q, k, v, log_f, s0):
    b, h, l, _ = q.shape
    dv = v.shape[-1]
    n = l // HG_CHUNK
    rs = lambda t: t.reshape(b, h, n, HG_CHUNK, t.shape[-1])
    q, k, v, log_f = rs(q), rs(k), rs(v), rs(log_f)
    cum = jnp.cumsum(log_f, axis=3)
    ref = cum[:, :, :, HG_CHUNK // 2 - 1:HG_CHUNK // 2, :]
    scores = jnp.einsum('bhnck,bhnsk->bhncs', q * jnp.exp(cum - ref), k * jnp.exp(ref - cum))
    tri = jnp.tril(jnp.ones((HG_CHUNK, HG_CHUNK), dtype=bool))
    scores = jnp.where(tri, scores, 0.0)
    intra = jnp.einsum('bhncs,bhnsv->bhncv', scores, v)
    last = cum[:, :, :, -1:, :]
    chunk_kv = jnp.einsum('bhnck,bhncv->nbhkv', k * jnp.exp(last - cum), v)
    chunk_decay = jnp.moveaxis(jnp.exp(last[:, :, :, 0, :]), 2, 0)

    def step(s, inp):
        dec, kv = inp
        return dec[..., None] * s + kv, s

    s_final, s_prev = lax.scan(step, s0, (chunk_decay, chunk_kv))
    inter = jnp.einsum('bhnck,nbhkv->bhncv', q * jnp.exp(cum), s_prev)
    return (intra + inter).reshape(b, h, l, dv), s_final

def _hgrn_inputs(h, w_in):
    q, v, zf, zb, g = jnp.split(h @ w_in, N_HG_PROJ, axis=-1)
    return jax.nn.silu(_heads(q)), _heads(v), _heads(zf), _heads(zb), g

def _hgrn_readout(o, g, gnorm, w_out):
    b, h, l, dv = o.shape
    o = o * lax.rsqrt(jnp.mean(o * o, axis=-1, keepdims=True) + EPS) * gnorm.astype(jnp.float32)
    o = o.transpose(0, 2, 1, 3).reshape(b, l, h * dv)
    y = (o * jax.nn.silu(g.astype(jnp.float32))).astype(g.dtype)
    return y @ w_out

def hgrn2_mixer(h_lat, h_ctx, w_in, lb_fwd, lb_bwd, gnorm, w_out, slot, need_ctx):
    lbf = _lower_bound(lb_fwd, slot)
    lbb = _lower_bound(lb_bwd, slot)
    qc, vc, zfc, zbc, gc = _hgrn_inputs(h_ctx, w_in)
    ql, vl, zfl, zbl, gl = _hgrn_inputs(h_lat, w_in)
    s0 = jnp.zeros((h_lat.shape[0], HG_HEADS, HG_EXPAND, HG_DV), jnp.float32)
    lf, kf = _gate(zfc, lbf)
    o_cf, s_f = _gla_scan(qc, kf, vc, lf, s0)
    lf, kf = _gate(zfl, lbf)
    o_lf, _ = _gla_scan(ql, kf, vl, lf, s_f)
    lbk, kb = _gate(zbc, lbb)
    o_cb, s_b = _gla_scan(_rev(qc), _rev(kb), _rev(vc), _rev(lbk), s0)
    lbk, kb = _gate(zbl, lbb)
    o_lb, _ = _gla_scan(_rev(ql), _rev(kb), _rev(vl), _rev(lbk), s_b)
    y_lat = _hgrn_readout(o_lf + _rev(o_lb), gl, gnorm, w_out)
    y_ctx = _hgrn_readout(o_cf + _rev(o_cb), gc, gnorm, w_out) if need_ctx else None
    return y_lat, y_ctx

def _box_sum(u, win, axis):
    n = u.shape[axis]
    cs = jnp.cumsum(u, axis=axis)
    pad = [(0, 0)] * u.ndim
    pad[axis] = (1, 0)
    cs = jnp.pad(cs, pad)
    t = jnp.arange(n)
    lo = jnp.clip(t - win // 2, 0, n)
    hi = jnp.clip(t - win // 2 + win, 0, n)
    return jnp.take(cs, hi, axis=axis) - jnp.take(cs, lo, axis=axis), hi - lo

def _grid_mean(u, win):
    b, l, d = u.shape
    rows = l // GRID_W
    g = u.reshape(b, rows, GRID_W, d)
    s, cnt_c = _box_sum(g, win, 2)
    s, cnt_r = _box_sum(s, win, 1)
    cnt = (cnt_r[:, None] * cnt_c[None, :]).astype(u.dtype)
    return (s / cnt[None, :, :, None]).reshape(b, l, d)

def _seq_mean(u, win):
    s, cnt = _box_sum(u, win, 1)
    return s / cnt.astype(u.dtype)[None, :, None]

def _pool_mix(h, mean_fn, w_in, w_grp, p_scale, w_out):
    u = (h @ w_in).astype(jnp.float32)
    parts = []
    for gi, win in enumerate(POOL_WINDOWS):
        ug = u[..., gi * POOL_GDIM:(gi + 1) * POOL_GDIM]
        parts.append((mean_fn(ug, win) - ug) @ w_grp[gi].astype(jnp.float32))
    y = jnp.concatenate(parts, axis=-1) * p_scale.astype(jnp.float32)
    return y.astype(h.dtype) @ w_out

def pool_mixer(h_lat, h_ctx, w_in, w_grp, p_scale, w_out, need_ctx):
    y_lat = _pool_mix(h_lat, _grid_mean, w_in, w_grp, p_scale, w_out)
    y_ctx = _pool_mix(h_ctx, _seq_mean, w_in, w_grp, p_scale, w_out) if need_ctx else None
    return y_lat, y_ctx

def moe_ffn(h, router_w, router_b, w_gate, w_up, w_down):
    n = h.shape[0]
    s = jax.nn.sigmoid((h @ router_w).astype(jnp.float32))
    sel = (s + router_b.astype(jnp.float32)).reshape(n, N_EXPERT_GROUPS, EXPERTS_PER_GROUP)
    top_v, top_i = lax.top_k(sel, TOP_K)
    best = jnp.argmax(jnp.sum(top_v, axis=-1), axis=-1)
    loc = jnp.take_along_axis(top_i, best[:, None, None], axis=1)[:, 0]
    ids = best[:, None] * EXPERTS_PER_GROUP + loc
    w = jnp.take_along_axis(s, ids, axis=1)
    w = w / jnp.sum(w, axis=-1, keepdims=True)
    combine = jnp.sum(jax.nn.one_hot(ids, N_EXPERTS, dtype=jnp.float32) * w[..., None], axis=1)
    y = jnp.zeros(h.shape, jnp.float32)
    for e in range(N_EXPERTS):
        a = jax.nn.silu(h @ w_gate[e]) * (h @ w_up[e])
        y = y + combine[:, e:e + 1] * (a @ w_down[e]).astype(jnp.float32)
    return y.astype(h.dtype)

def first_inputs(seed: int = 0) -> dict:
    key = jax.random.key(seed)
    ks = jax.random.split(key, 24)
    n_a = (DEPTH + N_MIXERS - 1) // N_MIXERS
    n_b = DEPTH // N_MIXERS
    nrm = lambda k, shape, sc: jax.random.normal(k, shape, jnp.float32) * sc
    d = D_MODEL
    return {
        "x": nrm(ks[0], (BATCH, SEQ, d), 1.0),
        "c": nrm(ks[1], (BATCH, d), 1.0),
        "ctx": nrm(ks[2], (BATCH, CTX_LEN, d), 1.0),
        "c_ctx": nrm(ks[3], (d,), 1.0),
        "w_mod": nrm(ks[4], (DEPTH, d, N_MOD * d), 0.5 * d ** -0.5),
        "b_mod": nrm(ks[5], (DEPTH, N_MOD * d), 0.01),
        "norm1_g": 1.0 + nrm(ks[6], (DEPTH, d), 0.05),
        "norm2_g": 1.0 + nrm(ks[7], (DEPTH, d), 0.05),
        "hg_w_in": nrm(ks[8], (n_a, d, N_HG_PROJ * d), d ** -0.5),
        "hg_lb_fwd": nrm(ks[9], (n_a + 1, d), 0.5),
        "hg_lb_bwd": nrm(ks[10], (n_a + 1, d), 0.5),
        "hg_gnorm": 1.0 + nrm(ks[11], (n_a, HG_DV), 0.05),
        "hg_w_out": nrm(ks[12], (n_a, d, d), d ** -0.5),
        "pool_w_in": nrm(ks[13], (n_b, d, d), d ** -0.5),
        "pool_w_grp": nrm(ks[14], (n_b, POOL_GROUPS, POOL_GDIM, POOL_GDIM), POOL_GDIM ** -0.5),
        "pool_scale": 1.0 + nrm(ks[15], (n_b, d), 0.1),
        "pool_w_out": nrm(ks[16], (n_b, d, d), d ** -0.5),
        "router_w": nrm(ks[17], (d, N_EXPERTS), d ** -0.5),
        "router_b": nrm(ks[18], (N_EXPERTS,), 0.01),
        "moe_w_gate": nrm(ks[19], (DEPTH, N_EXPERTS, d, D_EXPERT), d ** -0.5),
        "moe_w_up": nrm(ks[20], (DEPTH, N_EXPERTS, d, D_EXPERT), d ** -0.5),
        "moe_w_down": nrm(ks[21], (DEPTH, N_EXPERTS, D_EXPERT, d), D_EXPERT ** -0.5),
        "final_g": 1.0 + nrm(ks[22], (d,), 0.05),
    }

def first_block(x, c, ctx, c_ctx, w_mod, b_mod, norm1_g, norm2_g, hg_w_in, hg_lb_fwd, hg_lb_bwd, hg_gnorm,
              hg_w_out, pool_w_in, pool_w_grp, pool_scale, pool_w_out, router_w, router_b, moe_w_gate,
              moe_w_up, moe_w_down, final_g):
    x_lat, x_ctx = x, ctx
    d = x.shape[-1]
    for i in range(DEPTH):
        need_ctx = i < DEPTH - 1
        slot = i // N_MIXERS
        mod = jax.nn.silu(c) @ w_mod[i] + b_mod[i]
        sh1, sc1, g1, sh2, sc2, g2 = jnp.split(mod[:, None, :], N_MOD, axis=-1)
        mod_c = jax.nn.silu(c_ctx) @ w_mod[i] + b_mod[i]
        csh1, csc1, cg1, csh2, csc2, cg2 = jnp.split(mod_c, N_MOD, axis=-1)
        h_lat = modulate(x_lat, norm1_g[i], sh1, sc1)
        h_ctx = modulate(x_ctx, norm1_g[i], csh1, csc1)
        if i % N_MIXERS == 0:
            y_lat, y_ctx = hgrn2_mixer(h_lat, h_ctx, hg_w_in[slot], hg_lb_fwd, hg_lb_bwd, hg_gnorm[slot],
                                       hg_w_out[slot], slot, need_ctx)
        else:
            y_lat, y_ctx = pool_mixer(h_lat, h_ctx, pool_w_in[slot], pool_w_grp[slot], pool_scale[slot],
                                      pool_w_out[slot], need_ctx)
        x_lat = x_lat + g1 * y_lat
        h2_lat = modulate(x_lat, norm2_g[i], sh2, sc2).reshape(-1, d)
        n_lat = h2_lat.shape[0]
        if need_ctx:
            x_ctx = x_ctx + cg1 * y_ctx
            h2_ctx = modulate(x_ctx, norm2_g[i], csh2, csc2).reshape(-1, d)
            ff = moe_ffn(jnp.concatenate([h2_lat, h2_ctx], axis=0), router_w, router_b,
                         moe_w_gate[i], moe_w_up[i], moe_w_down[i])
            x_ctx = x_ctx + cg2 * ff[n_lat:].reshape(x_ctx.shape)
            ff_lat = ff[:n_lat]
        else:
            ff_lat = moe_ffn(h2_lat, router_w, router_b, moe_w_gate[i], moe_w_up[i], moe_w_down[i])
        x_lat = x_lat + g2 * ff_lat.reshape(x_lat.shape)
    return rms_norm(x_lat, final_g)


DEPTH_2 = 2

CHUNK = 64
N_CONV_LAYERS = (DEPTH_2 + 1) // 2
N_GDN_LAYERS = DEPTH_2 // 2
CONV_WIDTH = 3
GDN_HEADS = 8
GDN_HEAD_DIM = D_MODEL // GDN_HEADS
GDN_QK_DIM = GDN_HEADS * GDN_HEAD_DIM
GDN_V_DIM = GDN_HEADS * GDN_HEAD_DIM
GDN_CONV_WIDTH = 4
GDN_IN_DIM = 2 * GDN_QK_DIM + 2 * GDN_V_DIM + 2 * GDN_HEADS
N_GROUPS = 8
EXPERTS_PER_GROUP_2 = 8
N_EXPERTS_2 = N_GROUPS * EXPERTS_PER_GROUP_2
D_EXPERT_2 = D_MODEL // 4
D_SHARED = D_MODEL // 2
MOE_BLOCK = 128
NORM_EPS = 1e-6


def rmsnorm(x, w):
    xf = x.astype(jnp.float32)
    y = xf * lax.rsqrt(jnp.mean(xf * xf, axis=-1, keepdims=True) + NORM_EPS)
    return (y * w.astype(jnp.float32)).astype(x.dtype)

def l2norm(x):
    xf = x.astype(jnp.float32)
    return xf * lax.rsqrt(jnp.sum(xf * xf, axis=-1, keepdims=True) + NORM_EPS)

def causal_dwconv(x, w):
    K = w.shape[0]
    T = x.shape[1]
    xp = jnp.pad(x, ((0, 0), (K - 1, 0), (0, 0)))
    y = xp[:, 0:T] * w[0]
    for k in range(1, K):
        y = y + xp[:, k:k + T] * w[k]
    return y

def short_conv_mixer(h, w_in, conv_w, w_out):
    bcx = h @ w_in
    b, cg, xv = jnp.split(bcx, 3, axis=-1)
    y = b * causal_dwconv(cg * xv, conv_w)
    return y @ w_out

def chunk_gated_delta_rule(q, k, v, g, beta):
    out_dtype = v.dtype
    B, T, H, Dk = q.shape
    Dv = v.shape[-1]
    n = T // CHUNK

    def blocks(a):
        a = a.astype(jnp.float32).reshape((B, n, CHUNK, H) + a.shape[3:])
        return jnp.moveaxis(a, 3, 1)

    q, k, v, g, beta = (blocks(a) for a in (q, k, v, g, beta))
    gc = jnp.cumsum(g, axis=-1)
    idx = jnp.arange(CHUNK)
    causal = idx[:, None] >= idx[None, :]
    strict = idx[:, None] > idx[None, :]
    diff = gc[..., :, None] - gc[..., None, :]
    decay = jnp.exp(jnp.where(causal, diff, -jnp.inf))
    kb = k * beta[..., None]
    lower = jnp.where(strict, jnp.einsum('bhncd,bhnsd->bhncs', kb, k) * decay, 0.0)
    rhs = jnp.concatenate([v * beta[..., None], kb * jnp.exp(gc)[..., None]], axis=-1)
    sol = lax.linalg.triangular_solve(lower, rhs, left_side=True, lower=True,
                                      unit_diagonal=True)
    u, w = sol[..., :Dv], sol[..., Dv:]
    attn = jnp.einsum('bhncd,bhnsd->bhncs', q, k) * decay
    q_dec = q * jnp.exp(gc)[..., None]
    g_last = gc[..., -1]
    k_dec = k * jnp.exp(g_last[..., None] - gc)[..., None]

    def step(S, inp):
        u_n, w_n, qd_n, kd_n, a_n, gl_n = inp
        v_new = u_n - jnp.einsum('bhcd,bhde->bhce', w_n, S)
        o_n = (jnp.einsum('bhcd,bhde->bhce', qd_n, S)
               + jnp.einsum('bhcs,bhse->bhce', a_n, v_new))
        S = S * jnp.exp(gl_n)[..., None, None] + jnp.einsum('bhcd,bhce->bhde', kd_n, v_new)
        return S, o_n

    xs = tuple(jnp.moveaxis(a, 2, 0) for a in (u, w, q_dec, k_dec, attn, g_last))
    S0 = jnp.zeros((B, H, Dk, Dv), jnp.float32)
    _, o = lax.scan(step, S0, xs)
    o = jnp.transpose(o, (1, 0, 3, 2, 4)).reshape(B, T, H, Dv)
    return o.astype(out_dtype)

def gated_deltanet_mixer(h, w_in, conv_w, a_log, dt_bias, norm_w, w_out):
    B, T, _ = h.shape
    H, Dh = GDN_HEADS, GDN_HEAD_DIM
    proj = h @ w_in
    s1 = 2 * GDN_QK_DIM + GDN_V_DIM
    s2 = s1 + GDN_V_DIM
    qkv = proj[..., :s1]
    z = proj[..., s1:s2]
    b = proj[..., s2:s2 + H]
    a = proj[..., s2 + H:]
    qkv = jax.nn.silu(causal_dwconv(qkv, conv_w))
    q = qkv[..., :GDN_QK_DIM].reshape(B, T, H, Dh)
    k = qkv[..., GDN_QK_DIM:2 * GDN_QK_DIM].reshape(B, T, H, Dh)
    v = qkv[..., 2 * GDN_QK_DIM:].reshape(B, T, H, Dh)
    q = l2norm(q) * (Dh ** -0.5)
    k = l2norm(k)
    beta = jax.nn.sigmoid(b.astype(jnp.float32))
    g = -jnp.exp(a_log.astype(jnp.float32)) * jax.nn.softplus(
        a.astype(jnp.float32) + dt_bias.astype(jnp.float32))
    o = chunk_gated_delta_rule(q, k, v, g, beta)
    o = rmsnorm(o, norm_w) * jax.nn.silu(z.reshape(B, T, H, Dh))
    return o.reshape(B, T, GDN_V_DIM) @ w_out

def hier_moe(h, w_rg, b_rg, w_re, b_re, w_gate, w_up, w_down, ws_gate, ws_up, ws_down, w_sg):
    B, T, D = h.shape
    xt = h.reshape(-1, D)
    N = xt.shape[0]
    gl = (xt @ w_rg + b_rg).astype(jnp.float32)
    gp = jax.nn.softmax(gl, axis=-1)
    g_sel = jnp.argmax(gl, axis=-1)
    p_sel = jnp.take_along_axis(gp, g_sel[:, None], axis=-1)[:, 0]
    el = (xt @ w_re + b_re).astype(jnp.float32).reshape(N, N_GROUPS, EXPERTS_PER_GROUP_2)
    el_sel = jnp.take_along_axis(el, g_sel[:, None, None], axis=1)[:, 0]
    top_v, top_i = lax.top_k(el_sel, TOP_K)
    gate = jax.nn.softmax(top_v, axis=-1) * p_sel[:, None]
    eid = g_sel[:, None] * EXPERTS_PER_GROUP_2 + top_i
    S = N * TOP_K
    flat_e = eid.reshape(-1)
    flat_tok = jnp.repeat(jnp.arange(N), TOP_K)
    flat_gate = gate.reshape(-1)
    order = jnp.argsort(flat_e)
    e_sorted = flat_e[order]
    tok_sorted = flat_tok[order]
    gate_sorted = flat_gate[order].astype(xt.dtype)
    counts = jnp.bincount(flat_e, length=N_EXPERTS_2)
    starts = jnp.cumsum(counts) - counts
    padded = (counts + MOE_BLOCK - 1) // MOE_BLOCK * MOE_BLOCK
    pends = jnp.cumsum(padded)
    pstarts = pends - padded
    dest = pstarts[e_sorted] + (jnp.arange(S) - starts[e_sorted])
    n_blocks = -(-S // MOE_BLOCK) + N_EXPERTS_2
    P = n_blocks * MOE_BLOCK
    buf = jnp.zeros((P, D), xt.dtype).at[dest].set(xt[tok_sorted])
    block_e = jnp.minimum(
        jnp.searchsorted(pends, jnp.arange(n_blocks) * MOE_BLOCK, side='right'), N_EXPERTS_2 - 1)

    def expert_block(args):
        xb, e = args
        hid = jax.nn.silu(xb @ w_gate[e]) * (xb @ w_up[e])
        return hid @ w_down[e]

    out = lax.map(expert_block, (buf.reshape(n_blocks, MOE_BLOCK, D), block_e)).reshape(P, D)
    y = jnp.zeros((N, D), xt.dtype).at[tok_sorted].add(out[dest] * gate_sorted[:, None])
    ys = (jax.nn.silu(xt @ ws_gate) * (xt @ ws_up)) @ ws_down
    y = y + jax.nn.sigmoid(xt @ w_sg) * ys
    return y.reshape(B, T, D)

def second_inputs(seed: int = 0) -> dict:
    key = jax.random.key(seed)
    ks = jax.random.split(key, 32)
    D = D_MODEL
    nrm = jax.random.normal
    f32 = jnp.float32
    dt = jnp.exp(jax.random.uniform(ks[11], (N_GDN_LAYERS, GDN_HEADS), f32,
                                    np.log(1e-3), np.log(1e-1)))
    return {
        "x": nrm(ks[0], (BATCH, SEQ, D), f32),
        "c": nrm(ks[1], (BATCH, D), f32),
        "ada_w": nrm(ks[2], (DEPTH_2, D, 6 * D), f32) * (0.3 * D ** -0.5),
        "ada_b": nrm(ks[3], (DEPTH_2, 6 * D), f32) * 0.02,
        "norm_w": 1.0 + 0.05 * nrm(ks[4], (DEPTH_2, 4, D), f32),
        "conv_in_w": nrm(ks[5], (N_CONV_LAYERS, D, 3 * D), f32) * D ** -0.5,
        "conv_w": nrm(ks[6], (N_CONV_LAYERS, CONV_WIDTH, D), f32) * CONV_WIDTH ** -0.5,
        "conv_out_w": nrm(ks[7], (N_CONV_LAYERS, D, D), f32) * D ** -0.5,
        "gdn_in_w": nrm(ks[8], (N_GDN_LAYERS, D, GDN_IN_DIM), f32) * D ** -0.5,
        "gdn_conv_w": nrm(ks[9], (N_GDN_LAYERS, GDN_CONV_WIDTH, 2 * GDN_QK_DIM + GDN_V_DIM), f32) * 0.5,
        "gdn_a_log": jnp.log(jax.random.uniform(ks[10], (N_GDN_LAYERS, GDN_HEADS), f32, 1.0, 16.0)),
        "gdn_dt_bias": dt + jnp.log(-jnp.expm1(-dt)),
        "gdn_norm_w": 1.0 + 0.05 * nrm(ks[12], (N_GDN_LAYERS, GDN_HEAD_DIM), f32),
        "gdn_out_w": nrm(ks[13], (N_GDN_LAYERS, GDN_V_DIM, D), f32) * GDN_V_DIM ** -0.5,
        "moe_group_w": nrm(ks[14], (DEPTH_2, D, N_GROUPS), f32) * D ** -0.5,
        "moe_group_b": nrm(ks[15], (DEPTH_2, N_GROUPS), f32) * 0.01,
        "moe_expert_w": nrm(ks[16], (DEPTH_2, D, N_EXPERTS_2), f32) * D ** -0.5,
        "moe_expert_b": nrm(ks[17], (DEPTH_2, N_EXPERTS_2), f32) * 0.01,
        "moe_w_gate": nrm(ks[18], (DEPTH_2, N_EXPERTS_2, D, D_EXPERT_2), f32) * D ** -0.5,
        "moe_w_up": nrm(ks[19], (DEPTH_2, N_EXPERTS_2, D, D_EXPERT_2), f32) * D ** -0.5,
        "moe_w_down": nrm(ks[20], (DEPTH_2, N_EXPERTS_2, D_EXPERT_2, D), f32) * D_EXPERT_2 ** -0.5,
        "shared_w_gate": nrm(ks[21], (DEPTH_2, D, D_SHARED), f32) * D ** -0.5,
        "shared_w_up": nrm(ks[22], (DEPTH_2, D, D_SHARED), f32) * D ** -0.5,
        "shared_w_down": nrm(ks[23], (DEPTH_2, D_SHARED, D), f32) * D_SHARED ** -0.5,
        "shared_gate_w": nrm(ks[24], (DEPTH_2, D, 1), f32) * D ** -0.5,
    }

def second_block(x, c, ada_w, ada_b, norm_w, conv_in_w, conv_w, conv_out_w,
              gdn_in_w, gdn_conv_w, gdn_a_log, gdn_dt_bias, gdn_norm_w, gdn_out_w,
              moe_group_w, moe_group_b, moe_expert_w, moe_expert_b,
              moe_w_gate, moe_w_up, moe_w_down,
              shared_w_gate, shared_w_up, shared_w_down, shared_gate_w):
    cs = jax.nn.silu(c)
    for i in range(DEPTH_2):
        mod = (cs @ ada_w[i] + ada_b[i])[:, None, :]
        sh1, sc1, gt1, sh2, sc2, gt2 = jnp.split(mod, 6, axis=-1)
        h = rmsnorm(x, norm_w[i, 0]) * (1.0 + sc1) + sh1
        j = i // N_MIXERS
        if i % N_MIXERS == 0:
            y = short_conv_mixer(h, conv_in_w[j], conv_w[j], conv_out_w[j])
        else:
            y = gated_deltanet_mixer(h, gdn_in_w[j], gdn_conv_w[j], gdn_a_log[j],
                                     gdn_dt_bias[j], gdn_norm_w[j], gdn_out_w[j])
        x = x + gt1 * rmsnorm(y, norm_w[i, 1])
        h = rmsnorm(x, norm_w[i, 2]) * (1.0 + sc2) + sh2
        y = hier_moe(h, moe_group_w[i], moe_group_b[i], moe_expert_w[i], moe_expert_b[i],
                     moe_w_gate[i], moe_w_up[i], moe_w_down[i],
                     shared_w_gate[i], shared_w_up[i], shared_w_down[i], shared_gate_w[i])
        x = x + gt2 * rmsnorm(y, norm_w[i, 3])
    return x


def setup_inputs(seed=0):
    out = dict(first_inputs(seed))
    for name, value in second_inputs(seed + 1).items():
        if name != "x":
            out[name + "_2"] = value
    return out


def reference(
    x, c, ctx, c_ctx, w_mod, b_mod, norm1_g, norm2_g, hg_w_in, hg_lb_fwd, hg_lb_bwd, hg_gnorm,
    hg_w_out, pool_w_in, pool_w_grp, pool_scale, pool_w_out, router_w, router_b, moe_w_gate,
    moe_w_up, moe_w_down, final_g, c_2, ada_w_2, ada_b_2, norm_w_2, conv_in_w_2, conv_w_2,
    conv_out_w_2, gdn_in_w_2, gdn_conv_w_2, gdn_a_log_2, gdn_dt_bias_2, gdn_norm_w_2,
    gdn_out_w_2, moe_group_w_2, moe_group_b_2, moe_expert_w_2, moe_expert_b_2, moe_w_gate_2,
    moe_w_up_2, moe_w_down_2, shared_w_gate_2, shared_w_up_2, shared_w_down_2, shared_gate_w_2,
):
    x = first_block(
        x, c, ctx, c_ctx, w_mod, b_mod, norm1_g, norm2_g, hg_w_in, hg_lb_fwd, hg_lb_bwd,
        hg_gnorm, hg_w_out, pool_w_in, pool_w_grp, pool_scale, pool_w_out, router_w, router_b,
        moe_w_gate, moe_w_up, moe_w_down, final_g,
    )
    return second_block(
        x, c_2, ada_w_2, ada_b_2, norm_w_2, conv_in_w_2, conv_w_2, conv_out_w_2, gdn_in_w_2,
        gdn_conv_w_2, gdn_a_log_2, gdn_dt_bias_2, gdn_norm_w_2, gdn_out_w_2, moe_group_w_2,
        moe_group_b_2, moe_expert_w_2, moe_expert_b_2, moe_w_gate_2, moe_w_up_2, moe_w_down_2,
        shared_w_gate_2, shared_w_up_2, shared_w_down_2, shared_gate_w_2,
    )


_drawn_inputs = setup_inputs


def setup_inputs(seed=0):
    import zlib

    import numpy as np

    out = dict(_drawn_inputs(seed))
    spreads = {}
    factors = {'ctx': 27.267,
     'c_ctx': 6.793,
     'hg_lb_bwd': 2.975,
     'gdn_norm_w_2': 14.11,
     'moe_group_b_2': 5.052,
     'moe_expert_b_2': 5.57,
     'hg_lb_fwd': 4.157}
    for name, (base, spread) in spreads.items():
        noise = np.random.default_rng([zlib.crc32(name.encode()), seed]).standard_normal(out[name].shape)
        drawn = base * np.exp(spread * noise) if base else spread * noise
        out[name] = __import__('jax').numpy.asarray(drawn.astype(out[name].dtype))
    for name, factor in factors.items():
        out[name] = (out[name] * factor).astype(out[name].dtype)
    return out
```

```python
F = 1024
NTOK = 512
NCTX = 256
EPS = 1e-6


def program(nc, I, out):
    import concourse.bass as bass
    from concourse import mybir
    from contextlib import ExitStack

    f32 = mybir.dt.float32
    i32 = mybir.dt.int32
    ACT = mybir.ActivationFunctionType
    ALU = mybir.AluOpType
    AX = mybir.AxisListType.X

    ctx = ExitStack()
    ctx.__enter__()

    def sb(name, shape, dt=f32):
        return ctx.enter_context(nc.sbuf_tensor(name, shape, dt))

    def sem(name):
        return ctx.enter_context(nc.semaphore(name))

    class Queue:
        def __init__(self, name, chained):
            self.sem, self.n, self.ops, self.chained, self.first = sem(name), 0, [], chained, []
            self.outer = None

        def put(self, fn, waits=(), mark=True):
            waits = list(waits) + self.first
            self.first = []
            if self.chained and self.n:
                waits.append((self.sem, self.n))
            self.n += bool(mark)
            self.ops.append([fn, waits, (self.sem, 1) if mark else mark])
            return (self.sem, self.n)

        def last(self):
            if self.ops and self.ops[-1][0] is not None and self.ops[-1][2] is None:
                self.n += 1
                self.ops[-1][2] = (self.sem, 1)
            return (self.sem, self.n)

        def begin(self):
            self.last()
            self.outer, self.ops, self.before = self.ops, [], self.n

        def end(self, over):
            self.last()
            made = [(self.sem, self.before, self.n - self.before)] if self.n > self.before else []
            made += [(i[2][0], i[3], 16) for i in self.ops if i[2] and i[2][1] == 16 and i[3] is not None]
            self.outer.append([None, over, self.ops, made])
            self.ops, self.outer = self.outer, None

    PEQ, VEQ, ACQ, GPQ = Queue("s_pe", False), Queue("s_ve", True), Queue("s_ac", True), Queue("s_gp", True)
    SPQ = Queue("s_sp", False)
    QS = (SPQ, PEQ, VEQ, GPQ, ACQ)

    class Dma:

        def __init__(self, name, queue, n, once=False):
            self.q, self.sems, self.n, self.once = queue, [sem(f"{name}{i}") for i in range(n)], 0, once

        def put(self, fn, waits=()):
            s = self.sems[self.n % len(self.sems)]
            turn = self.n // len(self.sems)
            self.n += 1
            waits = list(waits) + ([(s, 16 * turn)] if turn else [])
            if self.q.chained and self.q.n:
                waits.append((self.q.sem, self.q.n))
            waits += self.q.first
            self.q.first = []
            self.q.ops.append([fn, waits, (s, 16), None if self.once else 16 * turn])
            return (s, 16 * (turn + 1))

        def marks(self):
            k = len(self.sems)
            return [(s, 16 * ((self.n - i + k - 1) // k)) for i, s in enumerate(self.sems) if self.n > i]

    RINGN = 8
    RD = Dma("d_ring", SPQ, RINGN)
    LD = Dma("d_ld", SPQ, 12)
    AD = Dma("d_act", ACQ, 4)
    GD = Dma("d_gp", GPQ, 8)

    def V(fn, *w):
        return VEQ.put(fn, w)

    def A(fn, *w):
        return ACQ.put(fn, w)

    def G(fn, *w):
        return GPQ.put(fn, w)

    def mm(o, l, r, st, sp, *w):
        PEQ.put(lambda e: e.matmul(o, l, r, start=st, stop=sp), w, mark=None)

    def tr(o, i, *w):
        PEQ.put(lambda e: e.transpose(o, i, ident[:, :]), w, mark=None)

    def act(o, i, f, *w, **kw):
        return A(lambda e: e.activation(o, i, f, **kw), *w)

    def tables():
        ACQ.put(lambda e: e.preload_act_table_set("natural_log_exp_and_others"), mark=False)

    def tt(Q, o, a, b, op, *w):
        return Q(lambda e: e.tensor_tensor(o, a, b, op), *w)

    def ts(Q, o, a, s1, s2, op0, op1, *w):
        if s2 is None:
            return Q(lambda e: e.tensor_scalar(o, a, s1, None, op0), *w)
        return Q(lambda e: e.tensor_scalar(o, a, s1, s2, op0, op1), *w)

    def stt(o, a, s, b, op0, op1, *w):
        return V(lambda e: e.scalar_tensor_tensor(o, a, s, b, op0, op1), *w)

    def red(o, a, op, *w):
        return V(lambda e: e.tensor_reduce(o, a, AX, op), *w)

    def cp(Q, o, a, *w):
        return Q(lambda e: e.tensor_copy(o, a), *w)

    def barrier():
        marks = [q.last() for q in (PEQ, VEQ, ACQ, GPQ)] + LD.marks() + AD.marks() + GD.marks()
        for q in (PEQ, VEQ, ACQ, GPQ):
            q.first = q.first + [m for m in marks if m[1]]
        return marks

    ring = sb("ring", [128, RINGN * 2048])
    ar = sb("arena", [128, 32256])
    ident, ones, triS, b64 = (sb(n, [128, 128]) for n in ("ident", "ones", "triS", "b64"))
    mf = sb("mf", [128, 128])
    mfi, mbi = sb("mfi", [128, 128], i32), sb("mbi", [128, 128], i32)
    mbc, mbsc, idc = (sb(n, [128, 64]) for n in ("mbc", "mbsc", "idc"))
    levc = [sb(f"lev{n}", [128, 64]) for n in (8, 16, 32, 64)]
    smask = sb("smask", [128, 768])
    iota = sb("iota", [128, 128])
    thr = sb("thr", [128, 16])
    epsc = sb("epsc", [128, 2])
    tok1 = sb("tok1", [128, 4])
    cols = sb("cols", [128, 512])
    sc = sb("sc", [128, 24])
    mod1 = sb("mod1", [128, 96])
    mod2 = sb("mod2", [128, 96])
    nrm = sb("nrm", [128, 64])
    small = sb("small", [128, 256])
    lbc = sb("lbc", [128, 80])
    vec = sb("vec", [128, 432])
    PS = ctx.enter_context(nc.psum_tensor("PS", [128, 8, 512], f32))

    def view(off, *shape):
        n = 1
        for s in shape:
            n *= s
        v = ar[:, off:off + n]
        if len(shape) == 1:
            return v
        names = "abcd"[:len(shape)]
        return v.rearrange(f"p ({' '.join(names)}) -> p {' '.join(names)}", **dict(zip(names, shape)))

    def bc(a, *shape):
        return a.to_broadcast([a.shape[0], *shape])

    class Bank:
        def __init__(self, i):
            self.i, self.ap, self.free = i, PS[:, i, :], (VEQ.sem, 0)

    banks = [Bank(i) for i in range(8)]

    class Banks:

        def __init__(self, which):
            self.which, self.n = which, 0

        def get(self):
            self.n += 1
            return self.which[(self.n - 1) % len(self.which)]

    allb = Banks(banks)

    EXTRA = {8: 14336, 9: 29768}

    class Unit:
        done = None

    class Ring:
        def __init__(self, slots, held):
            self.slots, self.n, self.held = slots, 0, held

        def load(self, src, k, reg=None):
            s = self.slots[self.n % len(self.slots)]
            self.n += 1
            u = Unit()
            u.ap = (ring[:, s * 2048:(s + 1) * 2048] if s < RINGN else view(EXTRA[s], 2048)).rearrange("p (k n) -> p k n", k=k)
            before = self.held.get(s)
            self.held[s] = u
            waits = [lambda: before.done] if before else []
            dst = u.ap
            u.ready = RD.put(lambda e: e.dma_start(dst, src(e) if callable(src) else src), waits)
            return u

        def cols(self, w, c0):
            return self.load(w[:, c0:c0 + 256].rearrange("(k p) n -> p k n", p=128), 8)

    R = Ring(list(range(RINGN)), {})
    RA = Ring([6, 7], R.held)

    def fill(o, v):
        return G(lambda e: e.memset(o, v))

    def sel(o, i, pattern, base, cm, op=ALU.is_ge, fillv=0.0):
        return G(lambda e: e.affine_select(out=o, in_=i, pattern=pattern, compare_op=op, fill=fillv,
                                           base=base, channel_multiplier=cm))

    fill(ident[:, :], 0.0)
    fill(ones[:, :], 1.0)
    fill(epsc[:, 0:1], EPS)
    fill(epsc[:, 1:2], 128 * EPS)
    sel(ident[:, :], ident[:, :], [[-1, 128]], 0, 1, ALU.not_equal, 1.0)
    sel(triS[:, :], ones[:, :], [[1, 128]], -1, -1)

    def blockmask(o, b):
        v = o[:, :].rearrange("p (j b) -> p j b", b=b)
        sel(v, ones[:, :].rearrange("p (j b) -> p j b", b=b), [[-b, 128 // b], [0, b]], 0, 1)
        return sel(v, v, [[b, 128 // b], [0, b]], b - 1, -1)

    mb, mbs, *lev = (view(256 + 128 * i, 128) for i in range(6))
    blockmask(b64, 64)
    sel(mf[:, :], b64[:, :], [[1, 128]], 0, -1)
    sel(mb[:, :], b64[:, :], [[-1, 128]], 0, 1)
    sel(mbs[:, :], b64[:, :], [[-1, 128]], -1, 1)
    G(lambda e: e.tensor_copy(mfi[:, :], mf[:, :]))
    G(lambda e: e.tensor_copy(mbi[:, :], mb[:, :]))
    for m, b in zip(lev, (8, 16, 32, 64)):
        blockmask(m, b)
    for i in (3, 2, 1):
        tt(G, lev[i][:, :], lev[i][:, :], lev[i - 1][:, :], ALU.subtract)
    for o, m in zip((mbc, mbsc, idc, *levc), (mb, mbs, ident, *lev)):
        for half in (slice(0, 64), slice(64, 128)):
            cp(G, o[half, :], m[half, half])
    fill(smask[:, :], 1.0)
    fill(smask[:, :].rearrange("p (n c) -> p n c", c=64)[:, :, 0:1], 0.0)
    ioti = view(0, 128).bitcast(i32)
    G(lambda e: e.iota(ioti, pattern=[[1, 128]], base=0, channel_multiplier=0))
    cp(G, iota[:, :], ioti)
    G(lambda e: e.iota(ioti[:, 0:4], pattern=[[128, 4]], base=1, channel_multiplier=1))
    cp(G, tok1[:, :], ioti[:, 0:4])
    ts(G, thr[:, 0:8], iota[:, 1:9], 64.0, None, ALU.mult, None)
    ts(G, thr[:, 8:16], iota[:, 1:9], 128.0, None, ALU.mult, None)
    consts = GPQ.last()

    crep = [view(15104 + 256 * i, 8, 32) for i in range(2)]
    stage = view(16384, 4, 128)
    z0 = V(lambda e: e.memset(stage, 0.0))
    rows = lambda v: v.rearrange("(r p) -> r p", p=128)
    loads = []

    def stage_in(j, r, src):
        loads.append(LD.put(lambda e: e.dma_start(stage[r:r + src.shape[0], j, :], src), [z0]))

    BM, N1, N2, LF, LB, CC = 0, 48, 56, 64, 80, 96
    stage_in(0, BM, rows(I["b_mod"][0]))
    stage_in(0, N1, rows(I["norm1_g"][0]))
    stage_in(0, N2, rows(I["norm2_g"][0]))
    stage_in(0, LF, I["hg_lb_fwd"].rearrange("a (r p) -> (a r) p", p=128))
    stage_in(0, LB, I["hg_lb_bwd"].rearrange("a (r p) -> (a r) p", p=128))
    stage_in(0, CC, rows(I["c"][0]))
    stage_in(0, CC + 8, rows(I["c_ctx"]))
    stage_in(0, CC + 16, rows(I["c_2"][0]))
    stage_in(1, 0, I["ada_b_2"].rearrange("a (r p) -> (a r) p", p=128))
    stage_in(1, 96, I["conv_w_2"][0].rearrange("a (r p) -> (a r) p", p=128))
    stage_in(2, 0, I["gdn_conv_w_2"][0].rearrange("a (r p) -> (a r) p", p=128))
    stage_in(3, 0, I["norm_w_2"].rearrange("a b (r p) -> (a b r) p", p=128))
    stage_in(3, 64, rows(I["final_g"]))
    b0 = allb.get()
    for j in range(4):
        tr(b0.ap[:, j * 128:(j + 1) * 128], stage[:, j, :], consts, *loads)
    b0.free = act(cols[:, :], b0.ap, ACT.Copy, PEQ.last())
    colA, colB, colC, colD = (cols[:, j * 128:(j + 1) * 128] for j in range(4))
    silu_c = act(sc[:, :], colA[:, CC:CC + 24], ACT.Silu)
    tables()
    zc = [V(lambda e, o=o: e.memset(o, 0.0)) for o in crep][-1]
    cp(V, crep[0][:, :, 0:2], sc[:, 0:16].rearrange("p (v k) -> p k v", k=8), silu_c, zc)
    crep_done = cp(V, crep[1][:, :, 0], sc[:, 16:24])
    ROWV = {}
    at = 0
    vl = []
    for name, src in (("gnorm", I["hg_gnorm"][0]), ("gdn_norm", I["gdn_norm_w_2"][0]), ("rb", I["router_b"]),
                      ("gb0", I["moe_group_b_2"][0]), ("eb0", I["moe_expert_b_2"][0]),
                      ("gb1", I["moe_group_b_2"][1]), ("eb1", I["moe_expert_b_2"][1]),
                      ("alog", I["gdn_a_log_2"][0]), ("dt", I["gdn_dt_bias_2"][0])):
        n = src.shape[0]
        ROWV[name] = vec[:, at:at + n]
        vl.append(LD.put(lambda e, o=ROWV[name], s=src: e.dma_start(o, s.partition_broadcast(128))))
        at += n
    V(lambda e: e.memset(small[:, 128:129], 0.0), *vl, b0.free)

    mrows = [view(15616 + 256 * i, 256) for i in range(2)]
    mtmp = view(16128, 4)
    mcount = [0]
    mread = [(PEQ.sem, 0)] * 2

    def mod_unit(w, u, which, nv, bias, dest, turn, ring_):
        un = ring_.cols(w, 256 * u)
        b = turn.get()
        for r_ in range(2):
            for j in range(4):
                mm(b.ap[32 * j:32 * j + 32, 0:256], crep[which][:, 4 * r_ + j, :], un.ap[:, 4 * r_ + j, :],
                   r_ == 0, r_ == 1, un.ready, crep_done, b.free)
        un.done = PEQ.last()
        i = mcount[0] % 2
        mcount[0] += 1
        b.free = j = act(mrows[i], b.ap[:, 0:256], ACT.Copy, un.done, mread[i])
        b = turn.get()
        for f in range(2):
            tr(b.ap[:, f * 128:(f + 1) * 128], mrows[i][:, f * 128:(f + 1) * 128], j, b.free)
        mread[i] = pk = PEQ.last()
        t3 = mtmp[:, 0:2 * nv].rearrange("p (f v) -> p f v", v=nv)
        b.free = red(t3, b.ap[:, 0:256].rearrange("p (f j v) -> p f v j", j=4, v=32)[:, :, 0:nv, :], ALU.add, pk)
        return tt(V, dest[:, 2 * u:2 * u + 2, :], t3, bc(bias[:, 2 * u:2 * u + 2].unsqueeze(2), 2, nv), ALU.add)

    m1 = mod1[:, :].rearrange("p (f v) -> p f v", v=2)
    m2 = [mod2[:, 48 * i:48 * i + 48] for i in range(2)]

    xl = view(20480, 4, F)
    xc = view(24576, 2, F)
    jc = LD.put(lambda e: e.dma_start(xc, I["ctx"][0].rearrange("(t p) d -> p t d", p=128)))
    jl = LD.put(lambda e: e.dma_start(xl, I["x"][0].rearrange("(t p) d -> p t d", p=128)))
    for u in range(8):
        mod_unit(I["w_mod"][0], u, 0, 2, colA[:, BM:BM + 48], m1, allb, R)
    ABS1 = small[:, 0:48]

    def ab(dst, g, mod, ch):
        stt(dst[:, 0:8], mod[:, 8 * ch + 8:8 * ch + 16], 1.0, g, ALU.add, ALU.mult)
        return cp(V, dst[:, 8:16], mod[:, 8 * ch:8 * ch + 8])

    ab(ABS1[:, 0:16], colA[:, N1:N1 + 8], m1[:, :, 1], 0)
    ab1 = ab(ABS1[:, 16:32], colA[:, N1:N1 + 8], m1[:, :, 0], 0)

    def rstd_of(dst, tiles, n, scratch, *w):
        for i, t in enumerate(tiles):
            act(scratch, t, ACT.Square, *w, accum_out=dst[:, i:i + 1])
        return rsqrt(dst[:, 0:len(tiles)], n, ACQ.last())

    def rsqrt(s, n, *w):
        act(s, s, ACT.Ln, *w, scale=1.0 / n, bias=epsc[:, 0:1])
        return act(s, s, ACT.Exp, scale=-0.5)

    rs = small[:, 64:80]
    r = rstd_of(rs, [xc[:, t, :] for t in range(2)] + [xl[:, t, :] for t in range(4)], F, view(19456, F), jc, jl)
    for t in range(6):
        xt = xc[:, t, :] if t < 2 else xl[:, t - 2, :]
        xn_done = ts(V, xt, xt, rs[:, t:t + 1], None, ALU.mult, None, r)
    hT = view(0, 8, 768)
    for k in range(8):
        b, b2 = allb.get(), allb.get()
        for t in range(2):
            tr(b.ap[:, t * 128:(t + 1) * 128], xc[:, t, k * 128:(k + 1) * 128], xn_done, b.free)
        for t in range(4):
            tr(b2.ap[:, t * 128:(t + 1) * 128], xl[:, t, k * 128:(k + 1) * 128], b2.free)
        pk = PEQ.last()
        b.free = ts(V, hT[:, k, 0:256], b.ap[:, 0:256], ABS1[:, k:k + 1], ABS1[:, 8 + k:9 + k], ALU.mult, ALU.add, pk)
        b2.free = act(hT[:, k, 256:768], b2.ap, ACT.Identity, pk, ab1, scale=ABS1[:, 16 + k:17 + k], bias=ABS1[:, 24 + k:25 + k])
    nd, la, lbm, lt = (lbc[:, 16 * i:16 * i + 16] for i in range(4))
    for d, c0 in enumerate((LF, LB)):
        tt(V, nd[:, 8 * d:8 * d + 8], colA[:, c0 + 8:c0 + 16], colA[:, c0:c0 + 8], ALU.subtract)
    j = VEQ.last()
    act(lt, nd, ACT.Abs, j)
    act(lt, lt, ACT.Exp, scale=-1.0)
    j = act(lt, lt, ACT.Ln, bias=ones[:, 0:1])
    ts(V, la, nd, 0.0, None, ALU.max, None)
    tt(V, la, la, lt, ALU.add, j)
    tt(V, lbm, la, nd, ALU.subtract)
    ts(V, la, la, -1.0, None, ALU.mult, None)
    ts(V, lbm, lbm, -1.0, None, ALU.mult, None)
    barrier()

    w_in = I["hg_w_in"][0]
    v = view(6144, 6, F)
    sg = view(12288, 4, F)
    og = view(16384, 4, F)
    for u in range(4):
        un = R.cols(w_in, F + 256 * u)
        for p in range(3):
            b = allb.get()
            for t in (2 * p, 2 * p + 1):
                for k in range(8):
                    mm(b.ap[:, (t % 2) * 256:(t % 2) * 256 + 256], hT[:, k, t * 128:(t + 1) * 128], un.ap[:, k, :],
                       k == 0, k == 7, un.ready, b.free)
            pk = PEQ.last()
            b.free = cp(V, v[:, 2 * p:2 * p + 2, 256 * u:256 * u + 256], b.ap.rearrange("p (t n) -> p t n", t=2), pk)
        un.done = pk
    zrow = view(16384, F)
    zr = fill(zrow, 0.0)
    y_ds, zd = {}, []
    for ns, nv in ((16, 7), (32, 8)):
        y_ds[ns] = o = nc.dram_tensor(f"y_d{ns}", ((ns + nv) * 128, F), f32, kind="Internal").ap()
        zd.append(GD.put(lambda e, o=o, ns=ns, nv=nv: e.dma_start(
            o[ns * 128:, :].rearrange("(t p) d -> p t d", p=128), bc(zrow.unsqueeze(1), nv, F)), [zr]))
    P0 = 20480
    qt_, kt_, kd, qcz = [], [], [], []
    for o in (P0, 12288):
        qt_.append(view(o, 512))
        kt_.append(view(o + 512, 512))
        kd.append(view(o + 1024, 768))
        qcz.append(view(o + 1792, 8, 128))
    kdz = view(P0 + 2816, 12, 128)
    scT = [view(P0 + 4352, 4, 128), view(P0 + 4864, 4, 128)]
    Sall = view(P0 + 5376, 8, 128)
    Stm = view(P0 + 6400, 2, 128)
    qT = view(P0 + 6656, 512)
    T = [view(P0 + 7168 + 768 * i, 768) for i in range(6)]
    assert P0 + 7168 + 768 * 6 <= 32256
    zz = [G(lambda e, o=o: e.memset(o, 0.0)) for o in (qcz[0], qcz[1], kdz, scT[0], scT[1])][-1]
    dec = [small[:, 80:92], small[:, 160:172]]
    ch = lambda a: a.rearrange("p (n c) -> p n c", c=64)
    pb = Banks(banks[3:8])
    hgu = {}
    M_ = {}

    def step(g):
        next(g, None)

    def proj(it):
        h, d = it // 2, it % 2
        if it % 4 == 0:
            hgu["q"] = R.cols(w_in, 128 * h)
            hgu[0] = R.cols(w_in, 2 * F + 128 * h)
            hgu[1] = R.cols(w_in, 3 * F + 128 * h)
        off = 128 * (h % 2)
        un = hgu[d]
        for k in range(8):
            mm(banks[1].ap, un.ap[:, k, off:off + 128], hT[:, k, 256:768], k == 0, k == 7, un.ready, banks[1].free)
        yield
        for k in range(8):
            mm(banks[2].ap[:, 0:256], un.ap[:, k, off:off + 128], hT[:, k, 0:256], k == 0, k == 7, banks[2].free)
        un.done = PEQ.last()
        M_["z", it] = un.done
        yield
        if d == 0:
            un = hgu["q"]
            for k in range(8):
                mm(banks[0].ap, un.ap[:, k, off:off + 128], hT[:, k, 256:768], k == 0, k == 7, un.ready, banks[0].free)
            un.done = PEQ.last()
            M_["q", it] = un.done
        yield

    def elem(it):
        h, d = it // 2, it % 2
        c, i = 8 * d + h, it % 2
        was = [M_[x, it - 1] for x in ("ve", "ge")] if it else [zz]
        pe = M_.get(("pe", it - 2), zz)
        banks[2].free = act(T[0][:, 0:256], banks[2].ap[:, 0:256], ACT.Copy, M_["z", it], *was)
        banks[1].free = z = act(T[0][:, 256:768], banks[1].ap, ACT.Copy)
        if d == 0:
            M_["qT"] = banks[0].free = act(qT, banks[0].ap, ACT.Silu, M_["q", it], *was)
            tables()
        act(T[1], T[0], ACT.Abs)
        act(T[1], T[1], ACT.Exp, scale=-1.0)
        l1 = act(T[1], T[1], ACT.Ln, bias=ones[:, 0:1])
        ts(V, T[2], T[0], -1.0, 0.0, ALU.mult, ALU.max, z)
        yield
        sp = tt(V, T[2], T[2], T[1], ALU.add, l1)
        y = ts(V, T[4], T[2], -1.0, nd[:, c:c + 1], ALU.mult, ALU.add, *was)
        j = tt(G, T[3], T[2], T[0], ALU.add, sp)
        ya = act(T[1], T[4], ACT.Abs, y)
        act(T[1], T[1], ACT.Exp, scale=-1.0)
        l2 = act(T[1], T[1], ACT.Ln, bias=ones[:, 0:1])
        kk = act(T[3], T[3], ACT.Exp, j, scale=-1.0, bias=lbm[:, c:c + 1])
        ts(V, T[4], T[4], 0.0, la[:, c:c + 1], ALU.max, ALU.add, ya)
        yield
        tt(V, T[4], T[4], T[1], ALU.add, l2)
        o5, i4 = (T[5], T[4]) if d == 0 else (T[5][:, ::-1], T[4][:, ::-1])
        cum = V(lambda e: e.tensor_tensor_scan(o5, smask[:, :], i4, 0.0, ALU.mult, ALU.add))
        c5 = ch(T[5])
        ref = c5[:, 4:12, 31:32] if d == 0 else c5[:, 4:12, 32:33]
        end = c5[:, :, 63:64] if d == 0 else c5[:, :, 0:1]
        x0 = tt(V, ch(T[0][:, 0:512]), c5[:, 4:12, :], bc(ref, 8, 64), ALU.subtract, j)
        x4 = tt(G, ch(T[4]), bc(end, 12, 64), c5, ALU.subtract, cum)
        e1 = act(T[1][:, 0:512], T[0][:, 0:512], ACT.Exp, x0)
        e2 = act(T[0][:, 0:512], T[0][:, 0:512], ACT.Exp, scale=-1.0)
        e4 = act(T[2][:, 0:512], T[5][:, 256:768], ACT.Exp, j)
        M_["dec", it] = act(dec[i], end[:, :, 0], ACT.Exp, M_.get(("st", it - 2), zz))
        e3 = act(T[4], T[4], ACT.Exp, x4)
        yield
        tt(G, qt_[i], qT, T[1][:, 0:512], ALU.mult, e1, M_["qT"], pe)
        tt(V, kt_[i], T[3][:, 256:768], T[0][:, 0:512], ALU.mult, e2, kk, pe)
        q3, e3v = qT.rearrange("p (n b c) -> p n b c", b=2, c=64), T[2][:, 0:512].rearrange("p (n b c) -> p n b c", b=2, c=64)
        z4 = qcz[i].rearrange("p (n b) c -> p n b c", b=2)
        tt(V, z4[:, :, 0, 0:64], q3[:, :, 0, :], e3v[:, :, 0, :], ALU.mult, e4, M_["qT"])
        M_["ge", it] = tt(G, z4[:, :, 1, 64:128], q3[:, :, 1, :], e3v[:, :, 1, :], ALU.mult, e4)
        M_["ve", it] = tt(V, kd[i], T[3], T[4], ALU.mult, e3)
        yield

    def body(it):
        h, d = it // 2, it % 2
        i = it % 2
        hc = slice(128 * h, 128 * h + 128)
        pe = M_.get(("pe", it - 1), zz)
        made = (M_["ve", it], M_["ge", it])
        ba, bb = pb.get(), pb.get()
        for t in range(6):
            b = ba if t < 4 else bb
            tr(b.ap[:, (t % 4) * 128:(t % 4) * 128 + 128], kd[i][:, t * 128:(t + 1) * 128], b.free, *made)
        pk = PEQ.last()
        bs = pb.get()
        for p in range(4):
            mm(bs.ap[:, p * 128:(p + 1) * 128], kt_[i][:, p * 128:(p + 1) * 128], qt_[i][:, p * 128:(p + 1) * 128],
               True, True, bs.free)
        ps_ = PEQ.last()
        yield
        kz = kdz.rearrange("p (t b) c -> p t b c", b=2)
        a4, b4 = ba.ap.rearrange("p (t c) -> p t c", c=128), bb.ap[:, 0:256].rearrange("p (t c) -> p t c", c=128)
        cp(V, kz[0:64, 0:4, 0, :], a4[0:64], pk)
        ba.free = k1 = cp(V, kz[64:128, 0:4, 1, :], a4[64:128])
        act(kz[0:64, 4:6, 0, :], b4[0:64], ACT.Copy, pk)
        bb.free = k2 = act(kz[64:128, 4:6, 1, :], b4[64:128], ACT.Copy)
        m, o, src = (mfi, mbi)[d], scT[d], bs.ap.rearrange("p (t c) -> p t c", c=128)
        bs.free = sco = V(lambda e, o=o, m=m, src=src: e.copy_predicated(o, bc(m[:, :].unsqueeze(1), 4, 128), src), ps_)
        yield
        order = list(range(11)) if d == 0 else [3, 2, 1, 0] + list(range(11, 4, -1))
        prev = None
        for s0 in (0, 4, 8):
            b = pb.get()
            part = order[s0:s0 + 4]
            for x_, n in enumerate(part):
                mm(b.ap[:, x_ * 128:(x_ + 1) * 128], kdz[:, n, :], v[:, n // 2, hc], True, True, k1, k2, b.free)
            pk = PEQ.last()
            for x_, n in enumerate(part):
                s_ = s0 + x_
                kv = b.ap[:, x_ * 128:(x_ + 1) * 128]
                if s_ < 3:
                    dst = Stm[:, s_ % 2, :]
                else:
                    dst = Sall[:, s_ - 3 if d == 0 else 10 - s_, :]
                if s_ == 0:
                    st = cp(V, dst, kv, pk, pe)
                else:
                    st = stt(dst, prev, dec[i][:, n:n + 1], kv, ALU.mult, ALU.add, pk, M_["dec", it], pe)
                prev = dst
            b.free = st
        M_["st", it] = st
        yield
        b = pb.get()
        for p in range(4):
            o = b.ap[:, p * 128:(p + 1) * 128]
            mm(o, scT[d][:, p, :], v[:, 2 + p, hc], True, False, sco, b.free)
            for n in (2 * p, 2 * p + 1):
                mm(o, qcz[i][:, n, :], Sall[:, n, :], False, n % 2 == 1, st, *made)
        M_["pe", it] = pk = PEQ.last()
        yield
        b3 = b.ap.rearrange("p (t c) -> p t c", c=128)
        if d == 0:
            M_["o"] = b.free = act(og[:, :, hc], b3, ACT.Copy, pk, *zd)
        else:
            M_["o"] = b.free = tt(V, og[:, :, hc], og[:, :, hc], b3, ALU.add, pk, M_["o"])
        yield

    ada = [(-1, u) for u in range(8, 24)] + [(i, u) for i in range(2) for u in range(24)]

    def ada_units(n):
        for _ in range(n):
            i, u = ada.pop(0)
            if i < 0:
                mod_unit(I["w_mod"][0], u, 0, 2, colA[:, BM:BM + 48], m1, pb, RA)
            else:
                mod_unit(I["ada_w_2"][i], u, 1, 1, colB[:, 48 * i:48 * i + 48], m2[i].unsqueeze(2), pb, RA)

    R.slots, R.n = [0, 1, 2, 3, 4, 5], 0
    for it in (0, 1):
        for _ in proj(it):
            pass
        if it == 0:
            for _ in elem(0):
                pass
    for it in range(16):
        B = body(it)
        E = elem(it + 1) if it < 15 else iter(())
        P = proj(it + 2) if it < 14 else iter(())
        step(E)
        step(B)
        step(B)
        step(P)
        ada_units(2)
        step(E)
        step(B)
        step(P)
        ada_units(2)
        step(E)
        step(B)
        step(P)
        step(E)
        step(B)
    for u in range(4):
        un = R.cols(w_in, 4 * F + 256 * u)
        for p in range(2):
            b = allb.get()
            for t in (2 * p, 2 * p + 1):
                for k in range(8):
                    mm(b.ap[:, (t % 2) * 256:(t % 2) * 256 + 256], hT[:, k, 256 + t * 128:256 + (t + 1) * 128],
                       un.ap[:, k, :], k == 0, k == 7, un.ready, b.free)
            pk = PEQ.last()
            o = sg[:, 2 * p:2 * p + 2, 256 * u:256 * u + 256]
            b.free = act(o, b.ap.rearrange("p (t n) -> p t n", t=2), ACT.Silu, pk, M_["pe", 15])
        un.done = pk
    for t in range(4):
        o = sg[:, t, :].rearrange("p (h d) -> p h d", d=128)
        tt(G, o, o, bc(ROWV["gnorm"].unsqueeze(1), 8, 128), ALU.mult, ACQ.last())
    tables()
    ab(ABS1[:, 32:48], colA[:, N2:N2 + 8], m1[:, :, 0], 3)
    barrier()

    R.slots, R.n = list(range(RINGN)), 0
    hs = small[:, 96:128].rearrange("p (t h) -> p t h", h=8)
    oT = view(6144, 8, 512)
    x = view(0, 4, F)
    jx = LD.put(lambda e: e.dma_start(x, I["x"][0].rearrange("(t p) d -> p t d", p=128)), barrier())
    for t in range(4):
        sq = view(20480 + 1024 * t, F)
        j = act(sq, og[:, t, :], ACT.Square)
        red(hs[:, t, :], sq.rearrange("p (h d) -> p h d", d=128), ALU.add, j)
    j = rsqrt(small[:, 96:128], 128, VEQ.last())
    for t in range(4):
        o3 = og[:, t, :].rearrange("p (h d) -> p h d", d=128)
        tt(V, o3, o3, bc(hs[:, t, :].unsqueeze(2), 8, 128), ALU.mult, j)
        tt(V, og[:, t, :], og[:, t, :], sg[:, t, :], ALU.mult)

    def transposed(src, dst, *w, ab=None):
        last = []
        for k in range(8):
            b = allb.get()
            for t in range(4):
                tr(b.ap[:, t * 128:(t + 1) * 128], src[:, t, k * 128:(k + 1) * 128], b.free, *w)
            pk = PEQ.last()
            o = dst[:, k, :]
            if ab is None:
                b.free = act(o, b.ap, ACT.Copy, pk) if k % 2 else cp(V, o, b.ap, pk)
            elif k % 2:
                b.free = act(o, b.ap, ACT.Identity, pk, VEQ.last(), scale=ab[:, k:k + 1], bias=ab[:, 8 + k:9 + k])
            else:
                b.free = ts(V, o, b.ap, ab[:, k:k + 1], ab[:, 8 + k:9 + k], ALU.mult, ALU.add, pk)
            last.append(b.free)
        return last[-2:]

    def row_of(col, dst, diag, *w):
        d3 = diag.rearrange("p (k j) -> p k j", j=128)
        j = tt(V, d3, bc(ident[:, :].unsqueeze(1), 8, 128), bc(col.unsqueeze(2), 8, 128), ALU.mult, *w)
        for n in range(2):
            b = allb.get()
            mm(b.ap, ones[:, :], diag[:, n * 512:(n + 1) * 512], True, True, j, b.free)
            pk = PEQ.last()
            b.free = act(dst[:, n * 512:(n + 1) * 512], b.ap, ACT.Copy, pk)
        return b.free

    def out_proj(aT, w, kt, evac, *waits):
        for u in range(4):
            un = R.cols(w, 256 * u) if kt == 8 else None
            for p in range(2):
                b = allb.get()
                for t in (2 * p, 2 * p + 1):
                    for k in range(8):
                        mm(b.ap[:, (t % 2) * 256:(t % 2) * 256 + 256], aT[:, k, t * 128:(t + 1) * 128], un.ap[:, k, :],
                           k == 0, k == 7, un.ready, b.free, *waits)
                pk = PEQ.last()
                b.free = evac(u, p, b.ap.rearrange("p (t n) -> p t n", t=2), pk)
            un.done = pk

    mo = transposed(og, oT, VEQ.last())
    grow = view(25600, F)
    gr = row_of(m1[:, 16:24, 0], grow, view(26624, F))
    tmpo = view(27648, 2, 2, 256)
    cnt = [0]

    def add_gated(u, p, b, pk):
        o = tmpo[:, cnt[0] % 2]
        cnt[0] += 1
        fr = tt(V, o, b, bc(grow[:, 256 * u:256 * u + 256].unsqueeze(1), 2, 256), ALU.mult, pk, gr)
        xs = x[:, 2 * p:2 * p + 2, 256 * u:256 * u + 256]
        tt(V, xs, xs, o, ALU.add, jx)
        return fr

    out_proj(oT, I["hg_w_out"][0], 8, add_gated, *mo)
    barrier()

    xn_d = nc.dram_tensor("xn_d", (NTOK, F), f32, kind="Internal").ap()

    XN, H2T = view(4096, 4, F), view(8192, 8, 512)
    RT0 = 12288
    XG = [view(16384 + 1024 * i, F) for i in range(3)]
    XGT = [view(19456 + 1024 * i, 8, 128) for i in range(2)]
    SG = [view(21504 + 256 * i, 256) for i in range(2)]
    AA = [view(22016 + 256 * i, 256) for i in range(2)]
    AT = [view(22528 + 256 * i, 2, 128) for i in range(2)]
    YB = [view(23040 + 1024 * i, F) for i in range(2)]
    GROW, DIAG = view(25088, F), view(26112, F)
    SHA = view(27136, 4, 512)
    WR = view(29184, 8, 73)
    RTX = view(29768, 2048)
    RTY = view(31816, 64)

    def moe(layer, NE, ab, wg, wu, wd, shared, gate_col):
        G_ = 1 if layer < 0 else 2
        C, NS, NV = 128 // G_, NE // G_, (7, 8)[G_ - 1]
        NB, NOV, y_d = NS + NV, NV * G_, y_ds[NS]
        th = thr[:, 8:15] if G_ == 1 else thr[:, 0:7]
        NR = 16 if layer < 0 else 73
        rt = [RT0]

        def tmp(*shape, dt=None):
            n = 1
            for s in shape:
                n *= s
            o = view(rt[0], *shape)
            rt[0] += n
            assert rt[0] <= 14336
            return o if dt is None else o.bitcast(dt)

        wr = view(29184, 8 * NR).rearrange("p (k n) -> p k n", n=NR)
        pre = barrier()
        if layer < 0:
            jw = [LD.put(lambda e: e.dma_start(wr, I["router_w"].rearrange("(k p) n -> p k n", p=128)), pre)]
        else:
            jw = [LD.put(lambda e, o=o, s=s: e.dma_start(o, s.rearrange("(k p) n -> p k n", p=128), allow_slow_non_contiguous=True), pre)
                  for o, s in ((wr[:, :, 0:8], I["moe_group_w_2"][layer]), (wr[:, :, 8:72], I["moe_expert_w_2"][layer]),
                               (wr[:, :, 72:73], I["shared_gate_w_2"][layer]))]
        zx = [G(lambda e, o=o: e.memset(o, 0.0)) for o in XG][-1]
        r = rstd_of(rs, [x[:, t, :] for t in range(4)], F, DIAG)
        for t in range(4):
            xn = ts(V, XN[:, t, :], x[:, t, :], rs[:, t:t + 1], None, ALU.mult, None, r)
        xd = AD.put(lambda e: e.dma_start(xn_d.rearrange("(t p) d -> p t d", p=128), XN), [xn])
        h2 = transposed(XN, H2T, xn, ab=ab)
        b = allb.get()
        for t in range(4):
            for k in range(8):
                mm(b.ap[:, t * NR:(t + 1) * NR], H2T[:, k, t * 128:(t + 1) * 128], wr[:, k, :], k == 0, k == 7, b.free, *h2, *jw)
        pk = PEQ.last()
        L = tmp(4, NR)
        b3 = b.ap[:, 0:4 * NR].rearrange("p (t n) -> p t n", n=NR)
        BIG = 1024.0

        def first_max(a, n, g, oh, mx, cand):
            red(mx, a, ALU.max)
            tt(V, cand, a, bc(mx.unsqueeze(2), g, n), ALU.is_ge)
            stt(cand, cand, -BIG, bc(iota[:, 0:n].unsqueeze(1), g, n), ALU.mult, ALU.add)
            mn = RTY[:, 0:g]
            red(mn, cand, ALU.min)
            return tt(V, oh, cand, bc(mn.unsqueeze(2), g, n), ALU.is_equal)

        w12 = tmp(4, 2)
        oh1, oh2, el, cand = tmp(4, NE), tmp(4, NE), tmp(4, NE), tmp(4, NE)
        if layer < 0:
            j = act(L, b3, ACT.Exp, pk, scale=-1.0)
            b.free = j
            ts(V, L, L, 1.0, None, ALU.add, None, j)
            V(lambda e: e.reciprocal(L, L))
            tt(V, el, L, bc(ROWV["rb"].unsqueeze(1), 4, 16), ALU.add)
            e16 = el.rearrange("p t (g e) -> p (t g) e", e=4)
            o16, c16 = oh1.rearrange("p t (g e) -> p (t g) e", e=4), cand.rearrange("p t (g e) -> p (t g) e", e=4)
            t1, t2 = tmp(16), tmp(16)
            first_max(e16, 4, 16, o16, t1, c16)
            stt(c16, o16, -1e30, e16, ALU.mult, ALU.add)
            red(t2, c16, ALU.max)
            tt(V, t1, t1, t2, ALU.add)
            t3, mx4 = tmp(4, 4), tmp(4)
            first_max(t1.rearrange("p (t g) -> p t g", g=4), 4, 4, t3, mx4, t2.rearrange("p (t g) -> p t g", g=4))
            ng, eg, ohg = 4, 4, t3
        else:
            b.free = cp(V, L, b3, pk)
            gl, ohg, t3, mx4 = tmp(4, 8), tmp(4, 8), tmp(4, 8), tmp(4)
            tt(V, gl, L[:, :, 0:8], bc(ROWV[f"gb{layer}"].unsqueeze(1), 4, 8), ALU.add)
            tt(V, el, L[:, :, 8:72], bc(ROWV[f"eb{layer}"].unsqueeze(1), 4, 64), ALU.add)
            first_max(gl, 8, 4, ohg, mx4, t3)
            j = tt(V, gl, gl, bc(mx4.unsqueeze(2), 4, 8), ALU.subtract)
            j = act(gl, gl, ACT.Exp, j)
            psel = tmp(4)
            red(psel, gl, ALU.add, j)
            V(lambda e: e.reciprocal(psel, psel))
            sgate = tmp(4)
            j = act(sgate, L[:, :, 72], ACT.Exp, scale=-1.0)
            ts(V, sgate, sgate, 1.0, None, ALU.add, None, j)
            V(lambda e: e.reciprocal(sgate, sgate))
            ng, eg = 8, 8
        ts(V, ohg, ohg, -1.0, 1e30, ALU.add, ALU.mult)
        e32 = el.rearrange("p t (g e) -> p (t g) e", e=eg)
        tt(V, e32, e32, bc(ohg.rearrange("p t g -> p (t g)").unsqueeze(2), 4 * ng, eg), ALU.add)
        v1, v2 = tmp(4), tmp(4)
        first_max(el, NE, 4, oh1, v1, cand)
        stt(el, oh1, -2e30, el, ALU.mult, ALU.add)
        first_max(el, NE, 4, oh2, v2, cand)
        if layer < 0:
            for n, oh in enumerate((oh1, oh2)):
                tt(V, cand, oh, L, ALU.mult)
                red(w12[:, :, n], cand, ALU.add)
            tt(V, v1, w12[:, :, 0], w12[:, :, 1], ALU.add)
            V(lambda e: e.reciprocal(v1, v1))
            tt(V, w12, w12, bc(v1.unsqueeze(2), 4, 2), ALU.mult)
        else:
            j = tt(V, v2, v2, v1, ALU.subtract)
            j = act(v2, v2, ACT.Exp, j)
            ts(V, v1, v2, 1.0, None, ALU.add, None, j)
            V(lambda e: e.reciprocal(v1, v1))
            tt(V, w12[:, :, 0], v1, psel, ALU.mult)
            tt(V, w12[:, :, 1], w12[:, :, 0], v2, ALU.mult)
        M = el
        j = tt(V, M, oh1, oh2, ALU.add)
        b = allb.get()
        for t in range(5):
            o = b.ap[:, t * NE:(t + 1) * NE]
            for s in range(min(t, 3) + 1):
                mm(o, triS[:, :] if s == t else ones[:, :], M[:, s, :], s == 0, s == min(t, 3), j, b.free)
        pk = PEQ.last()
        nov, ove, ovs, cn = tmp(NE), tmp(NE), tmp(NE), tmp(NE)
        cp(V, cn, b.ap[:, 4 * NE:5 * NE], pk)
        big = RTX[:, 0:NE * 7].rearrange("p (e n) -> p e n", n=7)
        tt(V, big, bc(cn.unsqueeze(2), NE, 7), bc(th.unsqueeze(1), NE, 7), ALU.is_gt)
        red(nov, big, ALU.add)
        V(lambda e: e.tensor_tensor_scan(ove, ones[:, 0:NE], nov, 0.0, ALU.mult, ALU.add))
        tt(V, ovs, ove, nov, ALU.subtract)
        pp, ee, oo, bb, ff, hh = (tmp(4, 2) for _ in range(6))
        pos3 = b.ap[:, 0:4 * NE].rearrange("p (t n) -> p t n", n=NE)
        for n, oh in enumerate((oh1, oh2)):
            tt(V, cand, oh, pos3, ALU.mult)
            red(pp[:, :, n], cand, ALU.add)
            tt(V, cand, oh, bc(iota[:, 0:NE].unsqueeze(1), 4, NE), ALU.mult)
            red(ee[:, :, n], cand, ALU.add)
            tt(V, cand, oh, bc(ovs.unsqueeze(1), 4, NE), ALU.mult)
            red(oo[:, :, n], cand, ALU.add)
        b.free = VEQ.last()
        f8 = lambda a: a.rearrange("p t n -> p (t n)")
        big = RTX[:, 0:56].rearrange("p (e n) -> p e n", n=7)
        tt(V, big, bc(f8(pp).unsqueeze(2), 8, 7), bc(th.unsqueeze(1), 8, 7), ALU.is_ge)
        red(f8(bb), big, ALU.add)
        stt(pp, bb, -float(C), pp, ALU.mult, ALU.add)
        ts(V, ff, bb, 1.0, None, ALU.min, None)
        stt(oo, bb, float(NE - 1), oo, ALU.add, ALU.add)
        tt(V, oo, oo, ee, ALU.subtract)
        tt(V, oo, oo, ff, ALU.mult)
        tt(V, ee, ee, oo, ALU.add)
        if G_ == 2:
            hi = hh.bitcast(i32)
            cp(V, hi, ee)
            V(lambda e: e.tensor_single_scalar(hi, hi, 1, ALU.bitwise_and))
            cp(V, ff, hi)
            tt(V, ee, ee, ff, ALU.subtract)
            ts(V, ee, ee, 0.5, None, ALU.mult, None)
            stt(pp, ff, float(C), pp, ALU.mult, ALU.add)
        yi = tmp(4, 2, dt=i32)
        stt(yi, ee, 128.0, pp, ALU.mult, ALU.add)
        ohb = RTX[:, 0:8 * NB].rearrange("p (t n k) -> p t n k", n=2, k=NB)
        ohp = RTX[:, 8 * NB:8 * NB + 1024].rearrange("p (t n k) -> p t n k", n=2, k=128)
        ob3, op3 = ohb.rearrange("p t n k -> p (t n) k"), ohp.rearrange("p t n k -> p (t n) k")
        tt(V, ob3, bc(iota[:, 0:NB].unsqueeze(1), 8, NB), bc(f8(ee).unsqueeze(2), 8, NB), ALU.is_equal)
        o4 = RTX[:, 0:8 * NB].rearrange("p (t n) -> p t n", t=4)
        tt(V, o4, o4, bc(tok1[:, :].unsqueeze(2), 4, 2 * NB), ALU.mult)
        j = tt(V, op3, bc(iota[:, :].unsqueeze(1), 8, 128), bc(f8(pp).unsqueeze(2), 8, 128), ALU.is_equal)
        b = allb.get()
        for n in range(8):
            mm(b.ap[:, 0:NB], op3[:, n, :], ob3[:, n, :], n == 0, n == 7, j, b.free)
        pk = PEQ.last()
        tk, tz = tmp(NB), tmp(NB)
        idx = tmp(NB, dt=i32)
        cp(V, tk, b.ap[:, 0:NB], pk)
        b.free = VEQ.last()
        ts(V, tz, tk, 0.0, 5000.0, ALU.is_equal, ALU.mult)
        idx_done = stt(idx, tk, -1.0, tz, ALU.add, ALU.add)
        ei = tmp(NOV)
        eii = tmp(NOV, dt=i32)
        big = RTX[:, 0:NOV * NE].rearrange("p (j e) -> p j e", e=NE)
        tt(V, big, bc(ove.unsqueeze(1), NOV, NE), bc(iota[:, 0:NOV].unsqueeze(2), NOV, NE), ALU.is_le)
        red(ei, big, ALU.add)
        ts(V, eii, ei, float(NE - 1), None, ALU.min, None)
        nvi = tmp(1, dt=i32)
        ei_done = cp(V, nvi, ove[:, NE - 1:NE])
        gr = row_of(gate_col, GROW, DIAG)
        if layer < 0:
            gr = row_of(colD[:, 64:72], view(27136, F), DIAG, PEQ.last())

        def shared_steps():
            sgw, suw, sdw = shared
            u0 = Unit()
            u0.done = ei_done
            RS = Ring([8, 9], {8: u0, 9: u0})
            pair = [RS.cols(sgw, 0), RS.cols(suw, 0)]
            yield
            for p in range(2):
                ug, uu = pair
                for f in range(2):
                    o = SHA[:, 2 * p + f, :]
                    for un in pair:
                        b = allb.get()
                        for k in range(8):
                            mm(b.ap, un.ap[:, k, f * 128:(f + 1) * 128], H2T[:, k, :], k == 0, k == 7, un.ready, b.free)
                        un.done = pk = PEQ.last()
                        if un is ug:
                            b.free = act(o, b.ap, ACT.Silu, pk)
                        else:
                            b.free = sh = tt(V, o, o, b.ap, ALU.mult, pk, ACQ.last())
                        yield
                yield
                if p == 0:
                    pair = [RS.cols(sgw, 256), RS.cols(suw, 256)]
                else:
                    dn = [RS.load(sdw[256 * i:256 * i + 256, :].rearrange("(k p) n -> p k n", p=128), 2) for i in range(2)]
                yield
            for t in range(4):
                for n in range(2):
                    b = allb.get()
                    for k in range(4):
                        un = dn[k // 2]
                        mm(b.ap, SHA[:, k, t * 128:(t + 1) * 128], un.ap[:, k % 2, n * 512:(n + 1) * 512],
                           k == 0, k == 3, un.ready, b.free, sh)
                    pk = PEQ.last()
                    o = XN[:, t, n * 512:(n + 1) * 512]
                    b.free = ts(V, o, b.ap, sgate[:, t:t + 1], None, ALU.mult, None, pk, xd)
                    yield

        free = dict(xg=[zx] * 3, xgt=[zx] * 2, at=[zx] * 2, yb=[None] * 2, sg=[zx] * 2)
        gath, st = {}, {}

        OD = Dma(f"d_ov{layer + 1}_", GPQ, NV, once=True)

        def gather(n):
            i = n % 3
            gath[n] = (GD if n < NS else OD).put(lambda e: e.indirect_dma_start(
                out=XG[i], out_offset=None, in_=xn_d, in_offset=bass.IndirectOffsetOnAxis(ap=idx[:, n:n + 1], axis=0),
                bounds_check=NTOK - 1, oob_is_err=False), [idx_done, xd, free["xg"][i]])

        def turn(n):
            i = n % 2
            ba, bb = allb.get(), allb.get()
            for k in range(8):
                b = (ba, bb)[k // 4]
                tr(b.ap[:, (k % 4) * 128:(k % 4) * 128 + 128], XG[n % 3][:, k * 128:(k + 1) * 128], gath[n], b.free)
            pk = PEQ.last()
            free["xg"][n % 3] = pk
            for k in range(4):
                ba.free = ts(V, XGT[i][:, k, :], ba.ap[:, k * 128:(k + 1) * 128], ab[:, k:k + 1], ab[:, 8 + k:9 + k],
                             ALU.mult, ALU.add, pk, free["xgt"][i])
            for k in range(4, 8):
                bb.free = act(XGT[i][:, k, :], bb.ap[:, (k - 4) * 128:(k - 3) * 128], ACT.Identity, pk, free["xgt"][i],
                              scale=ab[:, k:k + 1], bias=ab[:, 8 + k:9 + k])
            st[n] = (ba.free, bb.free)

        regs, count = {}, {}

        def unit_srcs(n):
            out_ = []
            for u in range(G_ * n, G_ * n + G_):
                if u < NE:
                    srcs = [w[u].rearrange("(k p) n -> p k n", p=128) for w in (wg, wu, wd)]
                else:
                    jj = u - NE

                    def dyn(w, key, jj=jj):
                        def src(e):
                            if key == 0:
                                regs[jj] = e.value_load(eii[0:1, jj:jj + 1], min_val=0, max_val=NE - 1)
                            return w[bass.ds(regs[jj], 1)].rearrange("a (k p) n -> p (a k) n", p=128)
                        return src
                    srcs = [dyn(wg, 0), dyn(wu, 1), dyn(wd, 2)]
                out_.append(srcs)
            return out_

        units = {}

        def loads(n):
            srcs = unit_srcs(n)
            units[n] = [[R.load(srcs[h][w], (8, 8, 2)[w]) for h in range(G_)] for w in range(3)]

        hs2 = [slice(C * h, C * h + C) for h in range(G_)]

        def experts(n, more):
            i = n % 2
            gu, dd = units[n][0:2], units[n][2]
            bg, bu = allb.get(), allb.get()
            for w, b in enumerate((bg, bu)):
                for k in range(8):
                    for h in range(G_):
                        mm(b.ap[hs2[h], 0:256], XGT[i][:, k, hs2[h]], gu[w][h].ap[:, k, :],
                           k == 0, k == 7, gu[w][h].ready, b.free, *st[n])
                for h in range(G_):
                    gu[w][h].done = PEQ.last()
            free["xgt"][i] = pk = PEQ.last()
            bg.free = s = act(SG[i], bg.ap[:, 0:256], ACT.Silu, gu[0][0].done, free["sg"][i])
            bu.free = aa = tt(V, AA[i], SG[i], bu.ap[:, 0:256], ALU.mult, pk, s)
            free["sg"][i] = aa
            more()
            b = allb.get()
            for f in range(2):
                tr(b.ap[:, f * 128:(f + 1) * 128], AA[i][:, f * 128:(f + 1) * 128], aa, b.free)
            pk = PEQ.last()
            b.free = at = cp(V, AT[i], b.ap[:, 0:256].rearrange("p (f s) -> p f s", s=128), pk, free["at"][i])
            bn = [allb.get(), allb.get()]
            for f in range(2):
                b = bn[f]
                for k in range(2):
                    for h in range(G_):
                        mm(b.ap[hs2[h], :], AT[i][:, k, hs2[h]], dd[h].ap[:, k, f * 512:(f + 1) * 512],
                           k == 0, k == 1, dd[h].ready, b.free, at)
                PEQ.last()
            pk = PEQ.last()
            for h in range(G_):
                dd[h].done = pk
            free["at"][i] = pk
            before = [free["yb"][i]] if free["yb"][i] else []
            bn[0].free = e0 = cp(V, YB[i][:, 0:512], bn[0].ap, pk, *before)
            bn[1].free = e1 = act(YB[i][:, 512:1024], bn[1].ap, ACT.Copy, pk, *before)
            free["yb"][i] = AD.put(lambda e: e.dma_start(y_d[n * 128:(n + 1) * 128, :], YB[i]), [e0, e1])

        for n in range(3):
            gather(n)
        loads(0)
        loads(1)
        S = shared_steps() if shared is not None else iter(())
        next(S, None)
        turn(0)
        for n in range(NS):
            def more(n=n):
                if n + 3 < NS:
                    gather(n + 3)
                if n + 1 < NS:
                    turn(n + 1)
            experts(n, more)
            if n + 2 < NS:
                loads(n + 2)
            next(S, None)
        for _ in S:
            pass
        barrier()

        def fetch(e):
            count[e] = e.value_load(nvi[0:1, 0:1], min_val=0, max_val=NOV)

        for q in QS:
            q.put(fetch, [ei_done], mark=False)
        for j in range(NV):
            for q in QS:
                q.begin()
            gather(NS + j)
            loads(NS + j)
            turn(NS + j)
            experts(NS + j, lambda: None)
            for q in QS:
                q.end(lambda e, j=j: count[e] > G_ * j)
        tables()
        done = barrier()
        ybuf = [view(o + 1024 * i, F) for o in (8192, 16384) for i in range(4)]
        gm = [GD.put(lambda e, i=i: e.indirect_dma_start(
            out=ybuf[i], out_offset=None, in_=y_d, in_offset=bass.IndirectOffsetOnAxis(ap=yi[:, i // 2, i % 2:i % 2 + 1], axis=0),
            bounds_check=NB * 128 - 1, oob_is_err=False), done) for i in range(8)]
        for t in range(4):
            if shared is None:
                j = ts(V, XN[:, t, :], ybuf[2 * t], w12[:, t, 0:1], None, ALU.mult, None, gm[2 * t])
            else:
                j = stt(XN[:, t, :], ybuf[2 * t], w12[:, t, 0:1], XN[:, t, :], ALU.mult, ALU.add, gm[2 * t])
            j = stt(XN[:, t, :], ybuf[2 * t + 1], w12[:, t, 1:2], XN[:, t, :], ALU.mult, ALU.add, gm[2 * t + 1])
            if layer < 0:
                tt(V, XN[:, t, :], XN[:, t, :], GROW, ALU.mult, gr)
                j = tt(V, x[:, t, :], x[:, t, :], XN[:, t, :], ALU.add)
            ss = rs[:, t:t + 1]
            act(DIAG, x[:, t, :] if layer < 0 else XN[:, t, :], ACT.Square, j, accum_out=ss)
            rsqrt(ss, F)
        for t in range(4):
            if layer < 0:
                j = stt(x[:, t, :], x[:, t, :], rs[:, t:t + 1], view(27136, F), ALU.mult, ALU.mult, ACQ.last())
            else:
                j = stt(XN[:, t, :], XN[:, t, :], rs[:, t:t + 1], GROW, ALU.mult, ALU.mult, gr, ACQ.last())
                tt(V, x[:, t, :], x[:, t, :], XN[:, t, :], ALU.add)
        barrier()

    def post_norm(y, grow, gr, *w):
        r = rstd_of(rs, [y[:, t, :] for t in range(4)], F, DIAG, *w)
        for t in range(4):
            stt(y[:, t, :], y[:, t, :], rs[:, t:t + 1], grow, ALU.mult, ALU.mult, r, gr)
            j = tt(V, x[:, t, :], x[:, t, :], y[:, t, :], ALU.add)
        return j

    moe(-1, 16, ABS1[:, 32:48], I["moe_w_gate"][0], I["moe_w_up"][0], I["moe_w_down"][0], None, m1[:, 40:48, 0])

    abn = [[nrm[:, 32 * i + 16 * s:32 * i + 16 * s + 16] for s in range(2)] for i in range(2)]
    gts = [[small[:, 192 + 16 * i + 8 * s:200 + 16 * i + 8 * s] for s in range(2)] for i in range(2)]
    for i in range(2):
        for s in range(2):
            ab(abn[i][s], colD[:, 32 * i + 16 * s:32 * i + 16 * s + 8], m2[i], 3 * s)
            tt(V, gts[i][s], m2[i][:, 24 * s + 16:24 * s + 24], colD[:, 32 * i + 16 * s + 8:32 * i + 16 * s + 16], ALU.mult)

    def pre_norm(ab, dst):
        r = rstd_of(rs, [x[:, t, :] for t in range(4)], F, DIAG, VEQ.last())
        for t in range(4):
            j = ts(V, XN[:, t, :], x[:, t, :], rs[:, t:t + 1], None, ALU.mult, None, r)
        return transposed(XN, dst, j, ab=ab)

    h0 = pre_norm(abn[0][0], H2T)
    YT = view(12288, 8, 512)
    CG = [view(16384 + 512 * i, 512) for i in range(2)]
    U = [view(17408 + 512 * i, 512) for i in range(2)]
    wc = I["conv_in_w_2"][0]
    cw = lambda i, f: colB[:, 96 + 8 * i + f:97 + 8 * i + f]
    for p in range(4):
        us = [R.cols(wc, F * s + 256 * p) for s in (1, 2, 0)]
        for f in range(2):
            ft = 2 * p + f
            bs = [allb.get() for _ in range(3)]
            ms = []
            for un, b in zip(us, bs):
                for k in range(8):
                    mm(b.ap, un.ap[:, k, f * 128:(f + 1) * 128], H2T[:, k, :], k == 0, k == 7, un.ready, b.free, *h0)
                un.done = PEQ.last()
                ms.append(un.done)
            cg, u, y = CG[f], U[f], YT[:, ft, :]
            bs[0].free = j = act(cg, bs[0].ap, ACT.Copy, ms[0], VEQ.last())
            bs[1].free = tt(V, u, cg, bs[1].ap, ALU.mult, ms[1], j)
            ts(V, y, u, cw(2, ft), None, ALU.mult, None)
            stt(y[:, 1:512], u[:, 0:511], cw(1, ft), y[:, 1:512], ALU.mult, ALU.add)
            stt(y[:, 2:512], u[:, 0:510], cw(0, ft), y[:, 2:512], ALU.mult, ALU.add)
            bs[2].free = tt(V, y, y, bs[2].ap, ALU.mult, ms[2])
    gr = row_of(gts[0][0], GROW, DIAG)

    def keep_rows(u, p, b, pk):
        o = XN[:, 2 * p:2 * p + 2, 256 * u:256 * u + 256]
        return act(o, b, ACT.Copy, pk) if p else cp(V, o, b, pk)

    out_proj(YT, I["conv_out_w_2"][0], 8, keep_rows, VEQ.last())
    post_norm(XN, GROW, gr, VEQ.last())
    barrier()

    def moe2(i):
        moe(i, 64, abn[i][1], I["moe_w_gate_2"][i], I["moe_w_up_2"][i], I["moe_w_down_2"][i],
            (I["shared_w_gate_2"][i], I["shared_w_up_2"][i], I["shared_w_down_2"][i]), gts[i][1])

    moe2(0)

    x_d = nc.dram_tensor("x_d", (NTOK, F), f32, kind="Internal").ap()
    xs = AD.put(lambda e: e.dma_start(x_d.rearrange("(t p) d -> p t d", p=128), x), [VEQ.last()])
    hG = view(4096, 8, 512)
    r = rstd_of(rs, [x[:, t, :] for t in range(4)], F, DIAG, VEQ.last())
    for t in range(4):
        j = ts(V, x[:, t, :], x[:, t, :], rs[:, t:t + 1], None, ALU.mult, None, r, xs)
    hg_done = transposed(x, hG, j, ab=abn[1][0])
    barrier()
    wi = I["gdn_in_w_2"][0]
    z = view(0, 4, F)
    WBA = view(28672, 8, 16)
    jb = LD.put(lambda e: e.dma_start(WBA, wi[:, 4096:4112].rearrange("(k p) n -> p k n", p=128)), barrier())
    Uu = view(8192, 4, F)
    nwT = view(12288, 8, 512)
    qdT = view(16384, 8, 512)
    kde = view(20480, 4, F)
    atT = view(24576, 8, 256)
    tail = [28800]

    def tl(*shape):
        n = 1
        for s in shape:
            n *= s
        o = view(tail[0], *shape)
        tail[0] += n
        assert tail[0] <= 32256
        return o

    for u in range(4):
        un = R.cols(wi, 3 * F + 256 * u)
        for p in range(2):
            b = allb.get()
            for t in (2 * p, 2 * p + 1):
                for k in range(8):
                    mm(b.ap[:, (t % 2) * 256:(t % 2) * 256 + 256], hG[:, k, t * 128:(t + 1) * 128],
                       un.ap[:, k, :], k == 0, k == 7, un.ready, b.free, *hg_done)
            pk = PEQ.last()
            b.free = act(z[:, 2 * p:2 * p + 2, 256 * u:256 * u + 256], b.ap.rearrange("p (t n) -> p t n", t=2), ACT.Silu, pk)
        un.done = pk
    for t in range(4):
        o = z[:, t, :].rearrange("p (h d) -> p h d", d=128)
        tt(G, o, o, bc(ROWV["gdn_norm"].unsqueeze(1), 8, 128), ALU.mult, ACQ.last())
    tables()
    b = allb.get()
    for t in range(4):
        for k in range(8):
            mm(b.ap[:, t * 16:(t + 1) * 16], hG[:, k, t * 128:(t + 1) * 128], WBA[:, k, :], k == 0, k == 7, b.free, jb)
    pk = PEQ.last()
    ba = tl(4, 16)
    b.free = cp(V, ba, b.ap[:, 0:64].rearrange("p (t n) -> p t n", n=16), pk)
    beta, gg, g1, gc, gk, egc = (tl(4, 8) for _ in range(6))
    j = act(beta, ba[:, :, 0:8], ACT.Exp, b.free, scale=-1.0)
    ts(V, beta, beta, 1.0, None, ALU.add, None, j)
    V(lambda e: e.reciprocal(beta, beta))
    j = tt(V, gg, ba[:, :, 8:16], bc(ROWV["dt"].unsqueeze(1), 4, 8), ALU.add)
    act(g1, gg, ACT.Abs, j)
    act(g1, g1, ACT.Exp, scale=-1.0)
    j = act(g1, g1, ACT.Ln, bias=ones[:, 0:1])
    ts(V, gg, gg, 0.0, None, ALU.max, None, j)
    tt(V, gg, gg, g1, ALU.add, j)
    ea = tl(8)
    j = act(ea, ROWV["alog"], ACT.Exp)
    ts(V, ea, ea, -1.0, None, ALU.mult, None, j)
    j = tt(V, gg, gg, bc(ea.unsqueeze(1), 4, 8), ALU.mult)
    b = allb.get()
    g32 = gg.rearrange("p t h -> p (t h)")
    mm(b.ap[:, 0:32], mf[:, :], g32, True, True, j, b.free)
    mm(b.ap[:, 32:64], b64[:, :], g32, True, True)
    pk = PEQ.last()
    cp(V, gc.rearrange("p t h -> p (t h)"), b.ap[:, 0:32], pk)
    b.free = j = tt(V, gk.rearrange("p t h -> p (t h)"), b.ap[:, 32:64], gc.rearrange("p t h -> p (t h)"), ALU.subtract)
    act(gk, gk, ACT.Exp, j)
    j = act(egc, gc, ACT.Exp)
    tt(V, egc, egc, beta, ALU.mult, j)
    decs = tl(8, 8)
    bar = barrier()
    R.slots, R.n = [0, 1, 2, 3], 0
    tq = [0]

    def rtl(*shape):
        n = 1
        for s in shape:
            n *= s
        v_ = ring[:, 8192 + tq[0]:8192 + tq[0] + n]
        tq[0] += n
        assert tq[0] <= 8192
        if len(shape) == 1:
            return v_
        return v_.rearrange("p (a b) -> p a b", a=shape[0])

    held = [R.held[s] for s in (4, 5, 6, 7)]
    freed = [lambda u=u: u.done for u in held]
    for q in (VEQ, ACQ, GPQ):
        q.first = q.first + freed
    Ts = [[rtl(512) for _ in range(3)] for _ in range(2)]
    XP = rtl(512)
    bv, bk = rtl(4, 128), rtl(4, 128)
    DC, DS, NN, NT, P2, PT, P4, XQ, XX, MM, YY = (rtl(4, 64) for _ in range(11))
    GR = tl(512)
    RR = tl(512)
    gcw = lambda i, f: colC[:, 24 * i + f:24 * i + f + 1]
    gdu = {}
    HV = (slice(0, 64), slice(64, 128))
    b3 = lambda b: b.ap.rearrange("p (t c) -> p t c", c=128)
    c3 = lambda b: b.ap[:, 0:256].rearrange("p (t c) -> p t c", c=64)
    m3 = lambda m: bc(m[:, :].unsqueeze(1), 4, 64)
    pbk, sbk = Banks(banks[0:3]), Banks(banks[3:8])
    H_ = {}


    def pre(h):
        if h % 2 == 0:
            for s in range(3):
                gdu[s] = R.cols(wi, F * s + 128 * h)
        off = 128 * (h % 2)
        conv = []
        for s, dst in enumerate(Ts[h % 2]):
            un, ft = gdu[s], 8 * s + h
            b = pbk.get()
            for k in range(8):
                mm(b.ap, un.ap[:, k, off:off + 128], hG[:, k, :], k == 0, k == 7, un.ready, b.free)
                if k % 2:
                    un.done = pk = PEQ.last()
                    yield
            j = act(dst, b.ap, ACT.Copy, pk, *H_.get(("read", h - 2), []), scale=gcw(3, ft))
            for i in (2, 1, 0):
                w = 3 - i
                j = stt(dst[:, w:512], b.ap[:, 0:512 - w], gcw(i, ft), dst[:, w:512], ALU.mult, ALU.add, j)
            b.free = j
            conv.append(j)
        H_["conv", h] = conv
        yield

    def norm(h):
        conv = H_["conv", h]
        made = [act(dst, dst, ACT.Silu, j) for dst, j in zip(Ts[h % 2], conv)]
        tables()
        for n, (sc_, eb) in enumerate(((128.0, 1), (1.0, 0))):
            dst = Ts[h % 2][n]
            j = act(RR, dst, ACT.Square)
            b = pbk.get()
            mm(b.ap, ones[:, :], RR, True, True, j, b.free)
            pk = PEQ.last()
            yield
            b.free = act(GR, b.ap, ACT.Ln, pk, VEQ.last(), scale=sc_, bias=epsc[:, eb:eb + 1])
            j = act(GR, GR, ACT.Exp, scale=-0.5)
            made[n] = tt(V, dst, dst, GR, ALU.mult, j)
        H_["made", h] = made
        yield

    def quads(b, l, r_, *w):
        for t in range(4):
            for hv in HV:
                mm(b.ap[hv, t * 64:(t + 1) * 64], l[hv, t, :], r_[hv, t, :], True, True, b.free, *w)
        return PEQ.last()

    def turned(src, dst, *w):
        b = sbk.get()
        for t in range(4):
            for hv in HV:
                mm(b.ap[hv, t * 64:(t + 1) * 64], src[hv, t, :], ident[hv, hv], True, True, b.free, *w)
        pk = PEQ.last()
        b.free = act(dst, c3(b), ACT.Copy, pk, VEQ.last())
        return b.free

    def sol(h):
        hc = slice(128 * h, 128 * h + 128)
        TQ, TK, TV = Ts[h % 2]
        mq, mk, mv = H_["made", h]
        end = H_.get(("end", h - 1), bar[0])
        j = tt(G, XP.rearrange("p (t c) -> p t c", c=128), bc(mf[:, :].unsqueeze(1), 4, 128), bc(gg[:, :, h:h + 1], 4, 128), ALU.mult, end, *bar)
        b = sbk.get()
        mm(b.ap, ones[:, :], XP, True, True, j, b.free)
        pk = PEQ.last()
        yield
        for n, hv in enumerate(HV):
            j = tt(V, DC[hv], bc(gc[hv, :, h:h + 1], 4, 64), b3(b)[hv, :, 64 * n:64 * n + 64], ALU.subtract, pk, end)
        qd = act(qdT[:, h, :], b.ap, ACT.Exp, j)
        b.free = qd
        ts(V, DC, DC, 0.0, None, ALU.min, None)
        je = act(DC, DC, ACT.Exp, VEQ.last())
        cp(V, decs[:, h, :], qdT[:, h, 63:512:64], qd)
        jq = tt(G, qdT[:, h, :], qdT[:, h, :], TQ, ALU.mult, VEQ.last(), mq)
        bq, bk2 = sbk.get(), sbk.get()
        for b, l in ((bk2, TK), (bq, TQ)):
            for t in range(4):
                for n, hv in enumerate(HV):
                    c = slice(t * 128 + 64 * n, t * 128 + 64 * n + 64)
                    mm(b.ap[hv, t * 64:(t + 1) * 64], l[:, c], TK[:, c], True, True, mq, mk, b.free)
            PEQ.last()
        ps_ = PEQ.last()
        yield
        tt(V, DC, DC, m3(mbc), ALU.mult, je)
        tt(V, DS, DC, m3(mbsc), ALU.mult)
        tt(V, DS, DS, bc(beta[:, :, h:h + 1], 4, 64), ALU.mult)
        bk2.free = jn = tt(V, NN, c3(bk2), DS, ALU.mult, ps_)
        bq.free = j = tt(V, XQ, c3(bq), DC, ALU.mult)
        jt = turned(NN, NT, jn)
        bvr, bkr = sbk.get(), sbk.get()
        for b, src in ((bvr, TV), (bkr, TK)):
            for t in range(4):
                tr(b.ap[:, t * 128:(t + 1) * 128], src[:, t * 128:(t + 1) * 128], mv, b.free)
        pk = PEQ.last()
        H_["read", h] = [pk, jq]
        jd = tt(V, DC, NN, m3(levc[0]), ALU.mult)
        yield
        jdt = tt(V, PT, NT, m3(levc[0]), ALU.mult, jt)
        b, b2 = sbk.get(), sbk.get()
        p1 = quads(b, PT, DC, jd, jdt)
        b.free = j2 = act(P2, c3(b), ACT.Copy, p1)
        p2 = quads(b2, DC, PT)
        yield
        b2.free = j2t = cp(V, NT, c3(b2), p2)
        tt(V, XX, NT, m3(idc), ALU.add, end)
        b = sbk.get()
        p1 = quads(b, P2, NT, j2, j2t)
        b.free = j4 = act(P4, c3(b), ACT.Copy, p1)
        bvr.free = tt(V, bv, b3(bvr), bc(beta[:, :, h:h + 1], 4, 128), ALU.mult, pk, end)
        yield
        tt(V, XX, XX, P4, ALU.add, j4)
        b = sbk.get()
        p1 = quads(b, P2, P4, j4)
        tt(V, bk, b3(bkr), bc(egc[:, :, h:h + 1], 4, 128), ALU.mult, pk)
        bkr.free = rv = tt(V, kde[:, :, hc], b3(bkr), bc(gk[:, :, h:h + 1], 4, 128), ALU.mult)
        yield
        b.free = jx = tt(V, XX, XX, c3(b), ALU.add, p1)
        b = sbk.get()
        p1 = quads(b, DC, XX, jx)
        yield
        b.free = jm = tt(V, XX, XX, c3(b), ALU.subtract, p1)
        for i in (1, 2, 3):
            jmt = turned(XX, MM, jm)
            jl = tt(V, DC, NN, m3(levc[i]), ALU.mult)
            b = sbk.get()
            p1 = quads(b, DC, XX, jl)
            b.free = jy = cp(V, YY, c3(b), p1)
            yield
            b = sbk.get()
            p1 = quads(b, MM, YY, jmt, jy)
            if i == 1:
                turned(XQ, atT[:, h, :].rearrange("p (t c) -> p t c", c=64), j)
            yield
            b.free = jm = tt(V, XX, XX, c3(b), ALU.subtract, p1)
        b, b0, b1 = (sbk.get() for _ in range(3))
        for t in range(4):
            for hv in HV:
                mm(b.ap[hv, t * 128:(t + 1) * 128], XX[hv, t, :], bv[hv, t, :], True, True, jm, rv, b.free)
        pk = PEQ.last()
        b.free = act(Uu[:, :, hc], b3(b), ACT.Copy, pk)
        n4 = nwT[:, h, :].rearrange("p (t n c) -> p t n c", n=2, c=64)
        for n, b in enumerate((b0, b1)):
            for t in range(4):
                mm(b.ap[:, t * 64:(t + 1) * 64], bk[HV[n], t, :], XX[HV[n], t, :], True, True, b.free)
            pk = PEQ.last()
            b.free = act(n4[:, :, n, :], c3(b), ACT.Copy, pk, scale=-1.0)
        H_["end", h] = pk
        yield

    for g in (pre(0), norm(0), pre(1)):
        for _ in g:
            pass
    for h in range(8):
        N = norm(h + 1) if h < 7 else iter(())
        P = pre(h + 2) if h < 6 else iter(())
        for _ in sol(h):
            next(N, None)
            next(P, None)
        for g in (N, P):
            for _ in g:
                pass
    barrier()
    oR = view(4096, 4, F)
    S_, Sd, vn = (ring[:, 8192 + 1024 * i:9216 + 1024 * i] for i in range(3))
    s3 = lambda a: a.rearrange("p (h d) -> p h d", d=128)
    fill(S_, 0.0)
    jv = fill(vn, 0.0)
    js = jv
    two = [PS[:, 2 * i:2 * i + 2, :].rearrange("p a n -> p (a n)") for i in range(4)]
    fr = [[] for _ in range(4)]
    for n in range(8):
        p, off = n // 2, 64 * (n % 2)
        half = slice(off, off + 64)
        cs = slice(64 * n, 64 * n + 64)
        A_, B_, C_ = (0, 2, 1) if n % 2 == 0 else (3, 2, 1)
        hs_ = [slice(128 * h, 128 * h + 128) for h in range(8)]
        for h in range(8):
            mm(two[A_][half, hs_[h]], nwT[:, h, cs], S_[:, hs_[h]], True, True, js, jv, *fr[A_])
        pk = PEQ.last()
        jsd = tt(G, s3(Sd), s3(S_), bc(decs[:, :, n:n + 1], 8, 128), ALU.mult, js)
        jn = tt(V, vn[half, :], two[A_][half, :], Uu[half, p, :], ALU.add, pk)
        fr[A_] = [jn]
        for h in range(8):
            mm(two[B_][:, hs_[h]], kde[half, p, hs_[h]], vn[half, hs_[h]], True, True, jn, *fr[B_])
        pkv = PEQ.last()
        for h in range(8):
            mm(two[C_][half, hs_[h]], qdT[:, h, cs], S_[:, hs_[h]], True, False, *fr[C_])
            mm(two[C_][half, hs_[h]], atT[half, h, p * 64:(p + 1) * 64], vn[half, hs_[h]], False, True)
        po = PEQ.last()
        fr[C_] = [act(oR[half, p, :], two[C_][half, :], ACT.Copy, po)]
        js = tt(V, S_, Sd, two[B_], ALU.add, pkv, po, jsd)
        fr[B_] = [js]
        jv = po
    for b in banks:
        b.free = VEQ.last()
    barrier()
    OT = view(12288, 8, 512)
    for t in range(4):
        sq = view(20480 + 1024 * t, F)
        j = act(sq, oR[:, t, :], ACT.Square)
        red(hs[:, t, :], sq.rearrange("p (h d) -> p h d", d=128), ALU.add, j)
    j = rsqrt(small[:, 96:128], 128, VEQ.last())
    for t in range(4):
        o3 = oR[:, t, :].rearrange("p (h d) -> p h d", d=128)
        tt(V, o3, o3, bc(hs[:, t, :].unsqueeze(2), 8, 128), ALU.mult, j)
        jz = tt(V, oR[:, t, :], oR[:, t, :], z[:, t, :], ALU.mult)
    end = barrier()
    x2 = LD.put(lambda e: e.dma_start(x, x_d.rearrange("(t p) d -> p t d", p=128)), end)
    R.slots, R.n = [4, 5, 6, 7, 0, 1, 2, 3], 0
    for s in (4, 5, 6, 7):
        u = Unit()
        u.done = end
        R.held[s] = u
    mo = transposed(oR, OT, jz)
    j = barrier()
    gr = row_of(gts[1][0], GROW, DIAG)
    out_proj(OT, I["gdn_out_w_2"][0], 8, keep_rows, *mo)
    post_norm(XN, GROW, gr, VEQ.last(), x2)
    barrier()
    moe2(1)
    fin = AD.put(lambda e: e.dma_start(out[0].rearrange("(t p) d -> p t d", p=128), x), [VEQ.last()])

    block = ctx.enter_context(nc.Block())
    ends = AD.marks()

    def emit(q, tailw=()):
        def waits_of(eng, waits, seen):
            need = {}
            for w in waits:
                w = w() if callable(w) else w
                for s, n in (w if isinstance(w, list) else [w]):
                    if n > seen.get(s, 0):
                        need[s] = max(need.get(s, 0), n)
            for s, n in need.items():
                eng.wait_ge(s, n)
                seen[s] = n

        def run(eng, ops, seen):
            for op in ops:
                if op[0] is None:
                    _, over, inner, made = op
                    if not inner:
                        continue
                    with eng.If(over(eng)):
                        run(eng, inner, dict(seen))
                    with eng.Else():
                        for s, before, n in made:
                            if before:
                                eng.wait_ge(s, before)
                            eng.sem_inc(s, n)
                    continue
                fn, waits, inc = op[:3]
                waits_of(eng, waits, seen)
                i = fn(eng)
                if inc:
                    i.then_inc(*inc)

        def go(eng):
            run(eng, q.ops, {})
            for s, n in tailw:
                eng.wait_ge(s, n)
        return go

    block.sync(emit(SPQ))
    block.tensor(emit(PEQ))
    block.vector(emit(VEQ))
    block.gpsimd(emit(GPQ))
    block.scalar(emit(ACQ, ends))
    ctx.close()


_INS = ["x", "c", "ctx", "c_ctx", "w_mod", "b_mod", "norm1_g", "norm2_g", "hg_w_in", "hg_lb_fwd", "hg_lb_bwd",
        "hg_gnorm", "hg_w_out", "router_w", "router_b", "moe_w_gate", "moe_w_up", "moe_w_down", "final_g", "c_2",
        "ada_w_2", "ada_b_2", "norm_w_2", "conv_in_w_2", "conv_w_2", "conv_out_w_2", "gdn_in_w_2", "gdn_conv_w_2",
        "gdn_a_log_2", "gdn_dt_bias_2", "gdn_norm_w_2", "gdn_out_w_2", "moe_group_w_2", "moe_group_b_2",
        "moe_expert_w_2", "moe_expert_b_2", "moe_w_gate_2", "moe_w_up_2", "moe_w_down_2", "shared_w_gate_2",
        "shared_w_up_2", "shared_w_down_2", "shared_gate_w_2"]


def kernel(**inputs):
    import numpy as np
    import concourse.bacc as bacc
    from concourse import mybir
    from concourse.bass_utils import run_bass_kernel_spmd

    nc = bacc.Bacc("TRN2", target_bir_lowering=False, num_devices=1)
    arrays, aps = {}, {}
    for name in _INS:
        a = np.ascontiguousarray(inputs[name])
        arrays[f"in_{name}"] = a
        aps[name] = nc.dram_tensor(f"in_{name}", a.shape, mybir.dt.from_np(a.dtype), kind="ExternalInput").ap()
    out = nc.dram_tensor("out_0", (1, NTOK, F), mybir.dt.float32, kind="ExternalOutput").ap()
    program(nc, aps, out)
    r = run_bass_kernel_spmd(nc, [arrays], core_ids=[0])
    return r.results[0]["out_0"]
```

```python
F = 1024
NTOK = 512
NCTX = 256
EPS = 1e-6


def program(nc, I, out):
    import concourse.bass as bass
    from concourse import mybir
    from contextlib import ExitStack

    f32 = mybir.dt.float32
    i32 = mybir.dt.int32
    ACT = mybir.ActivationFunctionType
    ALU = mybir.AluOpType
    AX = mybir.AxisListType.X

    ctx = ExitStack()
    ctx.__enter__()

    def sb(name, shape, dt=f32):
        return ctx.enter_context(nc.sbuf_tensor(name, shape, dt))

    def sem(name):
        return ctx.enter_context(nc.semaphore(name))

    class Queue:
        def __init__(self, name, chained):
            self.sem, self.n, self.ops, self.chained, self.first = sem(name), 0, [], chained, []
            self.outer = []

        def put(self, fn, waits=(), mark=True):
            waits = list(waits) + self.first
            self.first = []
            if self.chained and self.n:
                waits.append((self.sem, self.n))
            self.n += bool(mark)
            self.ops.append([fn, waits, (self.sem, 1) if mark else mark, None])
            return (self.sem, self.n)

        def last(self):
            if self.ops and self.ops[-1][0] is not None and self.ops[-1][2] is None:
                self.n += 1
                self.ops[-1][2] = (self.sem, 1)
            return (self.sem, self.n)

        def begin(self):
            self.last()
            self.outer.append((self.ops, self.n))
            self.ops = []

        def end(self, over):
            self.last()
            outer, before = self.outer.pop()
            made = [(self.sem, before, self.n - before)] if self.n > before else []

            def dmas(ops):
                for i in ops:
                    if i[0] is None:
                        yield from dmas(i[2])
                    elif i[2] and i[3] is not None:
                        yield (i[2][0], i[3], 16)

            made += dmas(self.ops)
            outer.append([None, over, self.ops, made])
            self.ops = outer

    PEQ, VEQ, ACQ, GPQ = Queue("s_pe", False), Queue("s_ve", True), Queue("s_ac", True), Queue("s_gp", True)
    SPQ = Queue("s_sp", False)
    QS = (SPQ, PEQ, VEQ, GPQ, ACQ)

    class Dma:

        def __init__(self, name, queue, n, once=False):
            self.q, self.sems, self.n, self.once = queue, [sem(f"{name}{i}") for i in range(n)], 0, once

        def put(self, fn, waits=()):
            s = self.sems[self.n % len(self.sems)]
            turn = self.n // len(self.sems)
            self.n += 1
            waits = list(waits) + ([(s, 16 * turn)] if turn else [])
            if self.q.chained and self.q.n:
                waits.append((self.q.sem, self.q.n))
            waits += self.q.first
            self.q.first = []
            self.q.ops.append([fn, waits, (s, 16), None if self.once else 16 * turn])
            return (s, 16 * (turn + 1))

        def marks(self):
            k = len(self.sems)
            return [(s, 16 * ((self.n - i + k - 1) // k)) for i, s in enumerate(self.sems) if self.n > i]

    RINGN = 8
    RD = Dma("d_ring", SPQ, RINGN)
    LD = Dma("d_ld", SPQ, 12)
    AD = Dma("d_act", ACQ, 8)
    GD = Dma("d_gp", GPQ, 8)

    def V(fn, *w):
        return VEQ.put(fn, w)

    def A(fn, *w):
        return ACQ.put(fn, w)

    def G(fn, *w):
        return GPQ.put(fn, w)

    def mm(o, l, r, st, sp, *w):
        PEQ.put(lambda e: e.matmul(o, l, r, start=st, stop=sp), w, mark=None)

    def tr(o, i, *w):
        PEQ.put(lambda e: e.transpose(o, i, ident[:, :]), w, mark=None)

    def act(o, i, f, *w, **kw):
        return A(lambda e: e.activation(o, i, f, **kw), *w)

    def tables():
        ACQ.put(lambda e: e.preload_act_table_set("natural_log_exp_and_others"), mark=False)

    def tt(Q, o, a, b, op, *w):
        return Q(lambda e: e.tensor_tensor(o, a, b, op), *w)

    def ts(Q, o, a, s1, s2, op0, op1, *w):
        if s2 is None:
            return Q(lambda e: e.tensor_scalar(o, a, s1, None, op0), *w)
        return Q(lambda e: e.tensor_scalar(o, a, s1, s2, op0, op1), *w)

    def stt(o, a, s, b, op0, op1, *w):
        return V(lambda e: e.scalar_tensor_tensor(o, a, s, b, op0, op1), *w)

    def red(o, a, op, *w):
        return V(lambda e: e.tensor_reduce(o, a, AX, op), *w)

    def cp(Q, o, a, *w):
        return Q(lambda e: e.tensor_copy(o, a), *w)

    def barrier():
        marks = [q.last() for q in (PEQ, VEQ, ACQ, GPQ)] + LD.marks() + AD.marks() + GD.marks()
        for q in (PEQ, VEQ, ACQ, GPQ):
            q.first = q.first + [m for m in marks if m[1]]
        return marks

    f32r = mybir.dt.float32r
    second = {}
    AR0 = RINGN * 2048
    for at, n in ((2 * 2048, 2 * 2048), (4 * 2048, 4 * 2048), *((AR0 + o, 4096) for o in (6144, 8192, 12288, 16384, 18432, 20480, 27136)),
                  *((AR0 + o, 6144) for o in (0, 17408, 23552))):
        with nc.sbuf_tensor(f"before{at}", [128, at], f32):
            with nc.sbuf_tensor(f"second{at}", [128, n], f32r) as second[at]:
                pass
    ring = sb("ring", [128, RINGN * 2048])
    ar = sb("arena", [128, 32256])
    ident, ones, triS, b64 = (sb(n, [128, 128]) for n in ("ident", "ones", "triS", "b64"))
    mf = sb("mf", [128, 128])
    mfi, mbi = sb("mfi", [128, 128], i32), sb("mbi", [128, 128], i32)
    mbc, mbsc, idc = (sb(n, [128, 64]) for n in ("mbc", "mbsc", "idc"))
    levc = [sb(f"lev{n}", [128, 64]) for n in (8, 16, 32, 64)]
    smask = sb("smask", [128, 768])
    iota = sb("iota", [128, 128])
    thr = sb("thr", [128, 24])
    epsc = sb("epsc", [128, 2])
    tok1 = sb("tok1", [128, 4])
    wrt = sb("wrt", [128, 584])
    cols = sb("cols", [128, 512])
    sc = sb("sc", [128, 24])
    mod1 = sb("mod1", [128, 96])
    mod2 = sb("mod2", [128, 96])
    nrm = sb("nrm", [128, 64])
    small = sb("small", [128, 256])
    lbc = sb("lbc", [128, 80])
    vec = sb("vec", [128, 432])
    PS = ctx.enter_context(nc.psum_tensor("PS", [128, 8, 512], f32))

    def view(off, *shape):
        n = 1
        for s in shape:
            n *= s
        v = ar[:, off:off + n]
        if len(shape) == 1:
            return v
        names = "abcd"[:len(shape)]
        return v.rearrange(f"p ({' '.join(names)}) -> p {' '.join(names)}", **dict(zip(names, shape)))

    def part(off):
        return second[AR0 + off][:, :].rearrange("p (k n) -> p k n", k=8)

    def mm3(o, l, r, st, sp, *w):
        mm(o, l[0], r[0], st, False, *w)
        mm(o, l[1], r[0], False, False)
        mm(o, l[0], r[1], False, sp)

    def bc(a, *shape):
        return a.to_broadcast([a.shape[0], *shape])

    class Bank:
        def __init__(self, i):
            self.i, self.ap, self.free = i, PS[:, i, :], (VEQ.sem, 0)

    banks = [Bank(i) for i in range(8)]

    class Banks:

        def __init__(self, which):
            self.which, self.n = which, 0

        def get(self):
            self.n += 1
            return self.which[(self.n - 1) % len(self.which)]

    allb = Banks(banks)

    EXTRA = {8: 14336, 9: 29768}

    class Unit:
        done = None

    class Ring:
        def __init__(self, slots, held):
            self.slots, self.n, self.held = slots, 0, held

        def load(self, src, k, reg=None):
            s = self.slots[self.n % len(self.slots)]
            self.n += 1
            u = Unit()
            u.ap = (ring[:, s * 2048:(s + 1) * 2048] if s < RINGN else view(EXTRA[s], 2048)).rearrange("p (k n) -> p k n", k=k)
            before = self.held.get(s)
            self.held[s] = u
            waits = [lambda: before.done] if before else []
            dst = u.ap
            u.ready = RD.put(lambda e: e.dma_start(dst, src(e) if callable(src) else src), waits)
            return u

        def cols(self, w, c0):
            return self.load(w[:, c0:c0 + 256].rearrange("(k p) n -> p k n", p=128), 8)

    R = Ring(list(range(RINGN)), {})
    wread, wn = [[], []], [0]

    def two_parts_begin():
        R.slots, R.n = [0, 1, 2, 3], 0
        was = [lambda u=R.held[s]: u.done for s in (4, 5, 6, 7) if s in R.held]
        wread[:] = [was, was]

    def two_parts(un):
        i = wn[0] % 2
        wn[0] += 1
        hi, lo = (second[4 * 2048][:, (2 * i + j) * 2048:(2 * i + j + 1) * 2048].rearrange("p (k n) -> p k n", k=8) for j in range(2))
        jh = act(hi, un.ap, ACT.Copy, un.ready, *wread[i])
        un.done = tt(V, lo, un.ap, hi.bitcast(f32), ALU.subtract, jh, un.ready)
        return i, (hi, lo), (jh, un.done)

    def two_parts_end():
        for s_ in (4, 5, 6, 7):
            R.held[s_] = Unit()
            R.held[s_].done = PEQ.last()
        R.slots, R.n = [4, 5, 6, 7, 0, 1, 2, 3], 0
    RA = Ring([6, 7], R.held)

    def fill(o, v):
        return G(lambda e: e.memset(o, v))

    def sel(o, i, pattern, base, cm, op=ALU.is_ge, fillv=0.0):
        return G(lambda e: e.affine_select(out=o, in_=i, pattern=pattern, compare_op=op, fill=fillv,
                                           base=base, channel_multiplier=cm))

    fill(ident[:, :], 0.0)
    fill(ones[:, :], 1.0)
    fill(epsc[:, 0:1], EPS)
    fill(epsc[:, 1:2], 128 * EPS)
    jid = sel(ident[:, :], ident[:, :], [[-1, 128]], 0, 1, ALU.not_equal, 1.0)
    sel(triS[:, :], ones[:, :], [[1, 128]], -1, -1)

    def blockmask(o, b):
        v = o[:, :].rearrange("p (j b) -> p j b", b=b)
        sel(v, ones[:, :].rearrange("p (j b) -> p j b", b=b), [[-b, 128 // b], [0, b]], 0, 1)
        return sel(v, v, [[b, 128 // b], [0, b]], b - 1, -1)

    mb, mbs, *lev = (view(256 + 128 * i, 128) for i in range(6))
    blockmask(b64, 64)
    sel(mf[:, :], b64[:, :], [[1, 128]], 0, -1)
    sel(mb[:, :], b64[:, :], [[-1, 128]], 0, 1)
    sel(mbs[:, :], b64[:, :], [[-1, 128]], -1, 1)
    G(lambda e: e.tensor_copy(mfi[:, :], mf[:, :]))
    G(lambda e: e.tensor_copy(mbi[:, :], mb[:, :]))
    for m, b in zip(lev, (8, 16, 32, 64)):
        blockmask(m, b)
    for i in (3, 2, 1):
        tt(G, lev[i][:, :], lev[i][:, :], lev[i - 1][:, :], ALU.subtract)
    for o, m in zip((mbc, mbsc, idc, *levc), (mb, mbs, ident, *lev)):
        for half in (slice(0, 64), slice(64, 128)):
            cp(G, o[half, :], m[half, half])
    fill(smask[:, :], 1.0)
    fill(smask[:, :].rearrange("p (n c) -> p n c", c=64)[:, :, 0:1], 0.0)
    ioti = view(0, 128).bitcast(i32)
    G(lambda e: e.iota(ioti, pattern=[[1, 128]], base=0, channel_multiplier=0))
    cp(G, iota[:, :], ioti)
    G(lambda e: e.iota(ioti[:, 0:4], pattern=[[128, 4]], base=1, channel_multiplier=1))
    cp(G, tok1[:, :], ioti[:, 0:4])
    ts(G, thr[:, 0:16], iota[:, 1:17], 40.0, None, ALU.mult, None)
    ts(G, thr[:, 16:24], iota[:, 1:9], 128.0, None, ALU.mult, None)
    consts = GPQ.last()

    crep = [view(15104 + 256 * i, 8, 32) for i in range(2)]
    stage = view(16384, 4, 128)
    z0 = V(lambda e: e.memset(stage, 0.0))
    rows = lambda v: v.rearrange("(r p) -> r p", p=128)
    loads = []

    def stage_in(j, r, src):
        loads.append(LD.put(lambda e: e.dma_start(stage[r:r + src.shape[0], j, :], src), [z0]))

    xl = view(20480, 4, F)
    xc = view(24576, 2, F)
    jc = LD.put(lambda e: e.dma_start(xc, I["ctx"][0].rearrange("(t p) d -> p t d", p=128)))
    jl = LD.put(lambda e: e.dma_start(xl, I["x"][0].rearrange("(t p) d -> p t d", p=128)))
    BM, N1, N2, LF, LB, CC = 0, 48, 56, 64, 80, 96
    stage_in(0, BM, rows(I["b_mod"][0]))
    stage_in(0, N1, rows(I["norm1_g"][0]))
    stage_in(0, N2, rows(I["norm2_g"][0]))
    stage_in(0, LF, I["hg_lb_fwd"].rearrange("a (r p) -> (a r) p", p=128))
    stage_in(0, LB, I["hg_lb_bwd"].rearrange("a (r p) -> (a r) p", p=128))
    stage_in(0, CC, rows(I["c"][0]))
    stage_in(0, CC + 8, rows(I["c_ctx"]))
    stage_in(0, CC + 16, rows(I["c_2"][0]))
    stage_in(1, 0, I["ada_b_2"].rearrange("a (r p) -> (a r) p", p=128))
    stage_in(1, 96, I["conv_w_2"][0].rearrange("a (r p) -> (a r) p", p=128))
    stage_in(2, 0, I["gdn_conv_w_2"][0].rearrange("a (r p) -> (a r) p", p=128))
    stage_in(3, 0, I["norm_w_2"].rearrange("a b (r p) -> (a b r) p", p=128))
    stage_in(3, 64, rows(I["final_g"]))
    b0 = allb.get()
    for j in range(4):
        tr(b0.ap[:, j * 128:(j + 1) * 128], stage[:, j, :], jid, *loads)
    b0.free = act(cols[:, :], b0.ap, ACT.Copy, PEQ.last())
    colA, colB, colC, colD = (cols[:, j * 128:(j + 1) * 128] for j in range(4))
    silu_c = act(sc[:, :], colA[:, CC:CC + 24], ACT.Silu)
    tables()
    zc = [V(lambda e, o=o: e.memset(o, 0.0)) for o in crep][-1]
    cp(V, crep[0][:, :, 0:2], sc[:, 0:16].rearrange("p (v k) -> p k v", k=8), silu_c, zc)
    crep_done = cp(V, crep[1][:, :, 0], sc[:, 16:24])
    mrows = [view(15616 + 256 * i, 256) for i in range(2)]
    mtmp = view(16128, 4)
    mcount, mpend, mlast = [0], [], [None]
    mread = [(PEQ.sem, 0)] * 2

    def mod_unit(w, u, which, nv, bias, dest, turn, ring_):
        un = ring_.cols(w, 256 * u)
        b = turn.get()
        for r_ in range(2):
            for j in range(4):
                mm(b.ap[32 * j:32 * j + 32, 0:256], crep[which][:, 4 * r_ + j, :], un.ap[:, 4 * r_ + j, :],
                   r_ == 0, r_ == 1, un.ready, crep_done, b.free)
        un.done = PEQ.last()
        i = mcount[0] % 2
        mcount[0] += 1
        b.free = j = act(mrows[i], b.ap[:, 0:256], ACT.Copy, un.done, mread[i])
        mod_flush()
        mpend.append(lambda: mod_turn(i, j, u, nv, bias, dest, turn))

    def mod_flush():
        while mpend:
            mlast[0] = mpend.pop()()
        return mlast[0]

    def mod_turn(i, j, u, nv, bias, dest, turn):
        b = turn.get()
        for f in range(2):
            tr(b.ap[:, f * 128:(f + 1) * 128], mrows[i][:, f * 128:(f + 1) * 128], j, b.free)
        mread[i] = pk = PEQ.last()
        t3 = mtmp[:, 0:2 * nv].rearrange("p (f v) -> p f v", v=nv)
        b.free = red(t3, b.ap[:, 0:256].rearrange("p (f j v) -> p f v j", j=4, v=32)[:, :, 0:nv, :], ALU.add, pk)
        return tt(V, dest[:, 2 * u:2 * u + 2, :], t3, bc(bias[:, 2 * u:2 * u + 2].unsqueeze(2), 2, nv), ALU.add)

    m1 = mod1[:, :].rearrange("p (f v) -> p f v", v=2)
    m2 = [mod2[:, 48 * i:48 * i + 48] for i in range(2)]

    def rstd_of(dst, tiles, n, scratch, *w):
        for i, t in enumerate(tiles):
            act(scratch, t, ACT.Square, *w, accum_out=dst[:, i:i + 1])
        return rsqrt(dst[:, 0:len(tiles)], n, ACQ.last())

    def rsqrt(s, n, *w):
        act(s, s, ACT.Ln, *w, scale=1.0 / n, bias=epsc[:, 0:1])
        return act(s, s, ACT.Exp, scale=-0.5)

    rs = small[:, 64:80]
    r = rstd_of(rs, [xc[:, t, :] for t in range(2)] + [xl[:, t, :] for t in range(4)], F, view(19456, F), jc, jl)
    for t in range(6):
        xt = xc[:, t, :] if t < 2 else xl[:, t - 2, :]
        xn_done = ts(V, xt, xt, rs[:, t:t + 1], None, ALU.mult, None, r)
    for u in range(8):
        mod_unit(I["w_mod"][0], u, 0, 2, colA[:, BM:BM + 48], m1, allb, R)
    mod_flush()
    ABS1 = small[:, 0:48]

    def ab(dst, g, mod, ch):
        stt(dst[:, 0:8], mod[:, 8 * ch + 8:8 * ch + 16], 1.0, g, ALU.add, ALU.mult)
        return cp(V, dst[:, 8:16], mod[:, 8 * ch:8 * ch + 8])

    ROWV = {}
    at = 0
    for name, src in (("gnorm", I["hg_gnorm"][0]), ("gdn_norm", I["gdn_norm_w_2"][0]), ("rb", I["router_b"]),
                      ("gb0", I["moe_group_b_2"][0]), ("eb0", I["moe_expert_b_2"][0]),
                      ("gb1", I["moe_group_b_2"][1]), ("eb1", I["moe_expert_b_2"][1]),
                      ("alog", I["gdn_a_log_2"][0]), ("dt", I["gdn_dt_bias_2"][0])):
        n = src.shape[0]
        ROWV[name] = vec[:, at:at + n]
        LD.put(lambda e, o=ROWV[name], s=src: e.dma_start(o, s.partition_broadcast(128)))
        at += n

    ab(ABS1[:, 0:16], colA[:, N1:N1 + 8], m1[:, :, 1], 0)
    ab1 = ab(ABS1[:, 16:32], colA[:, N1:N1 + 8], m1[:, :, 0], 0)

    hT = view(0, 8, 768)
    for k in range(8):
        b, b2 = allb.get(), allb.get()
        for t in range(2):
            tr(b.ap[:, t * 128:(t + 1) * 128], xc[:, t, k * 128:(k + 1) * 128], xn_done, b.free)
        for t in range(4):
            tr(b2.ap[:, t * 128:(t + 1) * 128], xl[:, t, k * 128:(k + 1) * 128], b2.free)
        pk = PEQ.last()
        b.free = ts(V, hT[:, k, 0:256], b.ap[:, 0:256], ABS1[:, k:k + 1], ABS1[:, 8 + k:9 + k], ALU.mult, ALU.add, pk, consts)
        b2.free = act(hT[:, k, 256:768], b2.ap, ACT.Identity, pk, ab1, consts, scale=ABS1[:, 16 + k:17 + k], bias=ABS1[:, 24 + k:25 + k])
    w_in = I["hg_w_in"][0]
    two_parts_begin()
    R.slots, R.n = [0, 1], 1
    nxt = two_parts(R.cols(w_in, F))
    nd, la, lbm, lt = (lbc[:, 16 * i:16 * i + 16] for i in range(4))
    for d, c0 in enumerate((LF, LB)):
        tt(V, nd[:, 8 * d:8 * d + 8], colA[:, c0 + 8:c0 + 16], colA[:, c0:c0 + 8], ALU.subtract)
    j = VEQ.last()
    act(lt, nd, ACT.Abs, j)
    act(lt, lt, ACT.Exp, scale=-1.0)
    j = act(lt, lt, ACT.Ln, bias=ones[:, 0:1])
    ts(V, la, nd, 0.0, None, ALU.max, None)
    tt(V, la, la, lt, ALU.add, j)
    tt(V, lbm, la, nd, ALU.subtract)
    ts(V, la, la, -1.0, None, ALU.mult, None)
    ts(V, lbm, lbm, -1.0, None, ALU.mult, None)
    barrier()

    v = view(6144, 6, F)
    sg = view(12288, 4, F)
    og = view(16384, 4, F)
    h2 = part(17408), part(23552)
    jh2, hg2, jg2 = [], (part(0)[:, :, 256:768], second[2 * 2048][:, :].rearrange("p (k n) -> p k n", k=8)), []
    lowas = [R.held[s].done for s in (2, 3)]
    for k in range(8):
        jh = act(h2[0][:, k, :], hT[:, k, :], ACT.Copy)
        jh2.append((jh, tt(V, h2[1][:, k, :], hT[:, k, :], h2[0][:, k, :].bitcast(f32), ALU.subtract, jh)))
    for u in range(4):
        i, wp, jw = nxt
        if u < 3:
            nxt = two_parts(R.cols(w_in, F + 256 * u + 256))
        for p in range(3):
            b = allb.get()
            for t in (2 * p, 2 * p + 1):
                c = slice(t * 128, (t + 1) * 128)
                for k in range(8):
                    mm3(b.ap[:, (t % 2) * 256:(t % 2) * 256 + 256], (h2[0][:, k, c], h2[1][:, k, c]),
                        (wp[0][:, k, :], wp[1][:, k, :]), k == 0, k == 7, b.free, *jw, *jh2[k])
            pk = PEQ.last()
            if p == 2:
                wread[i] = [pk]
            b.free = cp(V, v[:, 2 * p:2 * p + 2, 256 * u:256 * u + 256], b.ap.rearrange("p (t n) -> p t n", t=2), pk)
        for k in (2 * u, 2 * u + 1):
            jg2.append((act(hg2[0][:, k, :], h2[0][:, k, 256:768].bitcast(f32), ACT.Copy, jh2[k][1]),
                        cp(V, hg2[1][:, k, :], h2[1][:, k, 256:768].bitcast(f32), *lowas)))
        mod_unit(I["w_mod"][0], 8 + u, 0, 2, colA[:, BM:BM + 48], m1, allb, R)
    mod_flush()
    two_parts_end()
    PEvg = PEQ.last()
    zrow = view(16384, F)
    zr = fill(zrow, 0.0)
    y_ds, zd = {}, []
    for ne, c_, nov, p in ((16, 128, 7, 128), (64, 40, 26, 104)):
        y_ds[ne] = o = nc.dram_tensor(f"y_d{ne}", ((ne + nov) * c_, F), f32, kind="Internal").ap()
        zd.append(GD.put(lambda e, o=o[ne * c_:, :], p=p: e.dma_start(
            o.rearrange("(t p) d -> p t d", p=p), bc(zrow[0:p].unsqueeze(1), o.shape[0] // p, F)), [zr]))
    P0 = 20480
    qt_, kt_, kd, qcz = [], [], [], []
    for o in (P0, 12288):
        qt_.append(view(o, 512))
        kt_.append(view(o + 512, 512))
        kd.append(view(o + 1024, 768))
        qcz.append(view(o + 1792, 8, 128))
    kdz = view(P0 + 2816, 12, 128)
    scT = [view(P0 + 4352, 4, 128), view(P0 + 4864, 4, 128)]
    Sall = view(P0 + 5376, 8, 128)
    Stm = view(P0 + 6400, 2, 128)
    qT = view(P0 + 6656, 512)
    T = [view(P0 + 7168 + 768 * i, 768) for i in range(6)]
    assert P0 + 7168 + 768 * 6 <= 32256
    zz = [G(lambda e, o=o: e.memset(o, 0.0), PEQ.last()) for o in (qcz[0], qcz[1], kdz, scT[0], scT[1])][-1]
    dec = [small[:, 80:92], small[:, 160:172]]
    ch = lambda a: a.rearrange("p (n c) -> p n c", c=64)
    hs = small[:, 96:128].rearrange("p (t h) -> p t h", h=8)
    pb = Banks(banks[3:8])
    hgu = {}
    M_ = {}

    def step(g):
        next(g, None)

    hraw = {key: ring[:, o:o + 1024].rearrange("p (k n) -> p k n", k=8)
            for key, o in ((0, 2048), ("q", 3072), (1, 6 * 2048))}
    hwas = {0: [lambda u=R.held[1]: u.done], "q": [lambda u=R.held[1]: u.done], 1: [PEvg]}
    h2p, h2was = {}, {5: [PEvg], 7: [PEvg]}
    for s_ in (5, 7):
        h2p[s_] = [second[4 * 2048][:, (s_ - 4) * 2048 + 1024 * i:(s_ - 4) * 2048 + 1024 * i + 1024].rearrange("p (k n) -> p k n", k=8)
                   for i in range(2)]

    def half(key, h):
        c0 = {"q": 0, 0: 2 * F, 1: 3 * F}[key] + 128 * h
        src = w_in[:, c0:c0 + 128].rearrange("(k p) n -> p k n", p=128)
        hgu[key] = RD.put(lambda e: e.dma_start(hraw[key], src), hwas[key])

    def split(key, slot):
        (hi, lo), raw = h2p[slot], hraw[key]
        jh = act(hi, raw, ACT.Copy, hgu[key], *h2was[slot])
        return jh, tt(V, lo, raw, hi.bitcast(f32), ALU.subtract, jh, hgu[key])

    def lat(bank, slot, js):
        hi, lo = h2p[slot]
        for k in range(8):
            mm3(bank.ap, (hi[:, k, :], lo[:, k, :]), (hg2[0][:, k, :], hg2[1][:, k, :]), k == 0, k == 7, *js, bank.free, *jg2[k])
        pk = PEQ.last()
        h2was[slot] = [pk]
        return pk

    def ahead(it):
        if it % 2 == 0:
            half("q", it // 2 + 1)
        half(it % 2, it // 2 + 1)

    hgj = {}

    def splits(it):
        hgj[it % 2] = split(it % 2, 5)
        if it % 2 == 0:
            hgj["q"] = split("q", 7)
            hwas["q"] = [hgj["q"][1]]

    def proj(it):
        h, d = it // 2, it % 2
        M_["zl", it] = lat(banks[1], 5, hgj[d])
        yield
        for k in range(8):
            mm(banks[2].ap[:, 0:256], hraw[d][:, k, :], hT[:, k, 0:256], k == 0, k == 7, hgu[d], banks[2].free)
        M_["z", it] = PEQ.last()
        hwas[d] = [M_["z", it]]
        yield
        if d == 0:
            M_["q", it] = lat(banks[0], 7, hgj["q"])
        yield

    def elem(it):
        h, d = it // 2, it % 2
        c, i = 8 * d + h, it % 2
        was = [M_[x, it - 1] for x in ("ve", "ge")] if it else [zz]
        pe = M_.get(("pe", it - 2), zz)
        banks[2].free = act(T[0][:, 0:256], banks[2].ap[:, 0:256], ACT.Copy, M_["z", it], *was)
        banks[1].free = z = act(T[0][:, 256:768], banks[1].ap, ACT.Copy)
        if d == 0:
            M_["qT"] = banks[0].free = act(qT, banks[0].ap, ACT.Silu, M_["q", it], *was)
            tables()
        act(T[1], T[0], ACT.Abs)
        act(T[1], T[1], ACT.Exp, scale=-1.0)
        l1 = act(T[1], T[1], ACT.Ln, bias=ones[:, 0:1])
        ts(V, T[2], T[0], -1.0, 0.0, ALU.mult, ALU.max, z)
        yield
        sp = tt(V, T[2], T[2], T[1], ALU.add, l1)
        y = ts(V, T[4], T[2], -1.0, nd[:, c:c + 1], ALU.mult, ALU.add, *was)
        j = tt(G, T[3], T[2], T[0], ALU.add, sp)
        ya = act(T[1], T[4], ACT.Abs, y)
        act(T[1], T[1], ACT.Exp, scale=-1.0)
        l2 = act(T[1], T[1], ACT.Ln, bias=ones[:, 0:1])
        kk = act(T[3], T[3], ACT.Exp, j, scale=-1.0, bias=lbm[:, c:c + 1])
        ts(V, T[4], T[4], 0.0, la[:, c:c + 1], ALU.max, ALU.add, ya)
        yield
        tt(V, T[4], T[4], T[1], ALU.add, l2)
        o5, i4 = (T[5], T[4]) if d == 0 else (T[5][:, ::-1], T[4][:, ::-1])
        cum = V(lambda e: e.tensor_tensor_scan(o5, smask[:, :], i4, 0.0, ALU.mult, ALU.add))
        c5 = ch(T[5])
        ref = c5[:, 4:12, 31:32] if d == 0 else c5[:, 4:12, 32:33]
        end = c5[:, :, 63:64] if d == 0 else c5[:, :, 0:1]
        x0 = tt(V, ch(T[0][:, 0:512]), c5[:, 4:12, :], bc(ref, 8, 64), ALU.subtract, j)
        x4 = tt(G, ch(T[4]), bc(end, 12, 64), c5, ALU.subtract, cum)
        e1 = act(T[1][:, 0:512], T[0][:, 0:512], ACT.Exp, x0)
        e2 = act(T[0][:, 0:512], T[0][:, 0:512], ACT.Exp, scale=-1.0)
        e4 = act(T[2][:, 0:512], T[5][:, 256:768], ACT.Exp, j)
        M_["dec", it] = act(dec[i], end[:, :, 0], ACT.Exp, M_.get(("st", it - 2), zz))
        e3 = act(T[4], T[4], ACT.Exp, x4)
        yield
        tt(G, qt_[i], qT, T[1][:, 0:512], ALU.mult, e1, M_["qT"], pe)
        tt(V, kt_[i], T[3][:, 256:768], T[0][:, 0:512], ALU.mult, e2, kk, pe)
        q3, e3v = qT.rearrange("p (n b c) -> p n b c", b=2, c=64), T[2][:, 0:512].rearrange("p (n b c) -> p n b c", b=2, c=64)
        z4 = qcz[i].rearrange("p (n b) c -> p n b c", b=2)
        tt(V, z4[:, :, 0, 0:64], q3[:, :, 0, :], e3v[:, :, 0, :], ALU.mult, e4, M_["qT"])
        M_["ge", it] = tt(G, z4[:, :, 1, 64:128], q3[:, :, 1, :], e3v[:, :, 1, :], ALU.mult, e4)
        M_["ve", it] = tt(V, kd[i], T[3], T[4], ALU.mult, e3)
        yield

    def body(it):
        h, d = it // 2, it % 2
        i = it % 2
        hc = slice(128 * h, 128 * h + 128)
        pe = M_.get(("pe", it - 1), zz)
        made = (M_["ve", it], M_["ge", it])
        ba, bb = pb.get(), pb.get()
        for t in range(6):
            b = ba if t < 4 else bb
            tr(b.ap[:, (t % 4) * 128:(t % 4) * 128 + 128], kd[i][:, t * 128:(t + 1) * 128], b.free, *made)
        pk = PEQ.last()
        bs = pb.get()
        for p in range(4):
            mm(bs.ap[:, p * 128:(p + 1) * 128], kt_[i][:, p * 128:(p + 1) * 128], qt_[i][:, p * 128:(p + 1) * 128],
               True, True, bs.free)
        ps_ = PEQ.last()
        yield
        kz = kdz.rearrange("p (t b) c -> p t b c", b=2)
        a4, b4 = ba.ap.rearrange("p (t c) -> p t c", c=128), bb.ap[:, 0:256].rearrange("p (t c) -> p t c", c=128)
        cp(V, kz[0:64, 0:4, 0, :], a4[0:64], pk)
        ba.free = k1 = cp(V, kz[64:128, 0:4, 1, :], a4[64:128])
        act(kz[0:64, 4:6, 0, :], b4[0:64], ACT.Copy, pk)
        bb.free = k2 = act(kz[64:128, 4:6, 1, :], b4[64:128], ACT.Copy)
        m, o, src = (mfi, mbi)[d], scT[d], bs.ap.rearrange("p (t c) -> p t c", c=128)
        bs.free = sco = V(lambda e, o=o, m=m, src=src: e.copy_predicated(o, bc(m[:, :].unsqueeze(1), 4, 128), src), ps_)
        yield
        order = list(range(11)) if d == 0 else [3, 2, 1, 0] + list(range(11, 4, -1))
        prev = None
        for s0 in (0, 4, 8):
            b = pb.get()
            part = order[s0:s0 + 4]
            for x_, n in enumerate(part):
                mm(b.ap[:, x_ * 128:(x_ + 1) * 128], kdz[:, n, :], v[:, n // 2, hc], True, True, k1, k2, b.free)
            pk = PEQ.last()
            for x_, n in enumerate(part):
                s_ = s0 + x_
                kv = b.ap[:, x_ * 128:(x_ + 1) * 128]
                if s_ < 3:
                    dst = Stm[:, s_ % 2, :]
                else:
                    dst = Sall[:, s_ - 3 if d == 0 else 10 - s_, :]
                if s_ == 0:
                    st = cp(V, dst, kv, pk, pe)
                else:
                    st = stt(dst, prev, dec[i][:, n:n + 1], kv, ALU.mult, ALU.add, pk, M_["dec", it], pe)
                prev = dst
            b.free = st
        M_["st", it] = st
        yield
        b = pb.get()
        for p in range(4):
            o = b.ap[:, p * 128:(p + 1) * 128]
            mm(o, scT[d][:, p, :], v[:, 2 + p, hc], True, False, sco, b.free)
            for n in (2 * p, 2 * p + 1):
                mm(o, qcz[i][:, n, :], Sall[:, n, :], False, n % 2 == 1, st, *made)
        M_["pe", it] = pk = PEQ.last()
        yield
        b3 = b.ap.rearrange("p (t c) -> p t c", c=128)
        if d == 0:
            M_["o"] = b.free = act(og[:, :, hc], b3, ACT.Copy, pk, *zd)
        else:
            b.free = j = tt(V, og[:, :, hc], og[:, :, hc], b3, ALU.add, pk, M_["o"])
            for t in range(4):
                M_["o"] = act(view(16256, 128), og[:, t, hc], ACT.Square, j, accum_out=hs[:, t, h:h + 1])
        yield

    ada = [(-1, u) for u in range(12, 24)] + [(i, u) for i in range(2) for u in range(24)]

    def ada_units(n):
        for _ in range(min(n, len(ada))):
            i, u = ada.pop(0)
            if i < 0:
                mod_unit(I["w_mod"][0], u, 0, 2, colA[:, BM:BM + 48], m1, pb, RA)
            else:
                mod_unit(I["ada_w_2"][i], u, 1, 1, colB[:, 48 * i:48 * i + 48], m2[i].unsqueeze(2), pb, RA)

    RA.slots = [0, 4]
    for key in (0, "q", 1):
        half(key, 0)
    splits(0)
    for _ in proj(0):
        pass
    ahead(0)
    splits(1)
    for _ in elem(0):
        pass
    for _ in proj(1):
        pass
    ahead(1)
    splits(2)
    ada_units(2)
    for it in range(16):
        B = body(it)
        E = elem(it + 1) if it < 15 else iter(())
        P = proj(it + 2) if it < 14 else iter(())
        if it == 15:
            assert not ada
            mod_flush()
            for s_ in (1, 2, 3, 5, 6, 7):
                R.held[s_] = Unit()
                R.held[s_].done = M_["z", 15]
            two_parts_begin()
            R.slots = [1, 0]
            nxt = two_parts(R.cols(w_in, 4 * F))
        step(E)
        step(B)
        ada_units(1)
        step(B)
        step(E)
        step(P)
        step(E)
        step(B)
        ada_units(1)
        step(P)
        step(E)
        if it < 13:
            splits(it + 3)
        ada_units(1)
        step(B)
        step(P)
        ada_units(1)
        step(B)
        if it < 12:
            ahead(it + 2)
    mod_flush()
    ab(ABS1[:, 32:48], colA[:, N2:N2 + 8], m1[:, :, 0], 3)
    barrier()
    def transposed2(src, dst, *w, ab=None, full=None):
        marks, jab, pend = [], VEQ.last(), []

        def rest():
            k, b, o, j = pend.pop(0)
            jh = act(dst[0][:, k, :], o, ACT.Copy, j)
            jl = tt(V, dst[1][:, k, :], o, dst[0][:, k, :].bitcast(f32), ALU.subtract, jh)
            if ab is None:
                b.free = jl
            marks.append((jh, jl))

        for k in range(8):
            b = allb.get()
            for t in range(4):
                tr(b.ap[:, t * 128:(t + 1) * 128], src[:, t, k * 128:(k + 1) * 128], b.free, *w)
            j = PEQ.last()
            o = b.ap
            if ab is not None:
                o = full[:, k, :]
                if k % 2:
                    b.free = j = act(o, b.ap, ACT.Identity, j, jab, scale=ab[:, k:k + 1], bias=ab[:, 8 + k:9 + k])
                else:
                    b.free = j = ts(V, o, b.ap, ab[:, k:k + 1], ab[:, 8 + k:9 + k], ALU.mult, ALU.add, j)
            pend.append((k, b, o, j))
            if k:
                rest()
        rest()
        return marks

    def transposed(src, dst, *w, ab=None, turn=allb, then=None):
        last, jab = [], VEQ.last()
        for k in range(8):
            b = turn.get()
            for t in range(4):
                tr(b.ap[:, t * 128:(t + 1) * 128], src[:, t, k * 128:(k + 1) * 128], b.free, *w)
            pk = PEQ.last()
            o = dst[:, k, :]
            if ab is None:
                b.free = act(o, b.ap, ACT.Copy, pk) if k % 2 else cp(V, o, b.ap, pk)
            elif k % 2:
                b.free = act(o, b.ap, ACT.Identity, pk, jab, scale=ab[:, k:k + 1], bias=ab[:, 8 + k:9 + k])
            else:
                b.free = ts(V, o, b.ap, ab[:, k:k + 1], ab[:, 8 + k:9 + k], ALU.mult, ALU.add, pk)
            last.append(b.free)
            if then and k:
                then(k - 1, last[-2])
        if then:
            then(7, last[-1])
        return last[-2:]

    def row_of(col, dst, diag, *w):
        d3 = diag.rearrange("p (k j) -> p k j", j=128)
        j = tt(G, d3, bc(ident[:, :].unsqueeze(1), 8, 128), bc(col.unsqueeze(2), 8, 128), ALU.mult, ACQ.last(), VEQ.last(), *w)
        for n in range(2):
            b = allb.get()
            mm(b.ap, ones[:, :], diag[:, n * 512:(n + 1) * 512], True, True, j, b.free)
            pk = PEQ.last()
            b.free = act(dst[:, n * 512:(n + 1) * 512], b.ap, ACT.Copy, pk)
        return b.free

    def out_proj(a, w, evac, marks, nxt=None):
        nxt = nxt or two_parts(R.cols(w, 0))
        for u in range(4):
            i, wp, jw = nxt
            if u < 3:
                nxt = two_parts(R.cols(w, 256 * u + 256))
            for p in range(2):
                b = allb.get()
                for t in (2 * p, 2 * p + 1):
                    c = slice(t * 128, (t + 1) * 128)
                    for k in range(8):
                        mm3(b.ap[:, (t % 2) * 256:(t % 2) * 256 + 256], (a[0][:, k, c], a[1][:, k, c]),
                            (wp[0][:, k, :], wp[1][:, k, :]), k == 0, k == 7, b.free, *jw, *marks[k])
                pk = PEQ.last()
                if p:
                    wread[i] = [pk]
                b.free = evac(u, p, b.ap.rearrange("p (t n) -> p t n", t=2), pk)

    abn = [[nrm[:, 32 * i + 16 * s:32 * i + 16 * s + 16] for s in range(2)] for i in range(2)]
    gts = [[small[:, 192 + 16 * i + 8 * s:200 + 16 * i + 8 * s] for s in range(2)] for i in range(2)]
    for i in range(2):
        for s in range(2):
            ab(abn[i][s], colD[:, 32 * i + 16 * s:32 * i + 16 * s + 8], m2[i], 3 * s)
            tt(V, gts[i][s], m2[i][:, 24 * s + 16:24 * s + 24], colD[:, 32 * i + 16 * s + 8:32 * i + 16 * s + 16], ALU.mult)

    oT = part(6144), part(20480)
    x = view(0, 4, F)
    grow = view(25600, F)
    gr = row_of(m1[:, 16:24, 0], grow, view(10240, F))
    j = rsqrt(small[:, 96:128], 128)
    for t in range(4):
        o3 = og[:, t, :].rearrange("p (h d) -> p h d", d=128)
        tt(V, o3, o3, bc(hs[:, t, :].unsqueeze(2), 8, 128), ALU.mult, j)
        tt(V, o3, o3, bc(ROWV["gnorm"].unsqueeze(1), 8, 128), ALU.mult)
    mo, jg = [], []

    def turn_gated(u):
        for k in (2 * u, 2 * u + 1):
            b = allb.get()
            for t in range(4):
                tr(b.ap[:, t * 128:(t + 1) * 128], og[:, t, k * 128:(k + 1) * 128], b.free, *jg[u])
            pk = PEQ.last()
            jh = act(oT[0][:, k, :], b.ap, ACT.Copy, pk)
            b.free = tt(V, oT[1][:, k, :], b.ap, oT[0][:, k, :].bitcast(f32), ALU.subtract, jh)
            mo.append((jh, b.free))

    for u in range(4):
        i, wp, jw = nxt
        nxt = two_parts(R.cols(w_in, 4 * F + 256 * u + 256) if u < 3 else R.cols(I["hg_w_out"][0], 0))
        js = []
        for p in range(2):
            b = allb.get()
            for t in (2 * p, 2 * p + 1):
                c = slice(t * 128, (t + 1) * 128)
                for k in range(8):
                    mm3(b.ap[:, (t % 2) * 256:(t % 2) * 256 + 256], (hg2[0][:, k, c], hg2[1][:, k, c]),
                        (wp[0][:, k, :], wp[1][:, k, :]), k == 0, k == 7, b.free, *jw, *jg2[k])
            pk = PEQ.last()
            if p:
                wread[i] = [pk]
            c = slice(256 * u, 256 * u + 256)
            b.free = act(sg[:, 2 * p:2 * p + 2, c], b.ap.rearrange("p (t n) -> p t n", t=2), ACT.Silu, pk)
            js.append(tt(V, og[:, 2 * p:2 * p + 2, c], og[:, 2 * p:2 * p + 2, c], sg[:, 2 * p:2 * p + 2, c], ALU.mult, b.free))
        jg.append(js)
        if u:
            turn_gated(u - 1)
    for s_ in (2, 3):
        R.held[s_].done = PEQ.last()
    R.slots, R.n = [2, 3, 0, 1], 0
    jx = LD.put(lambda e: e.dma_start(x, I["x"][0].rearrange("(t p) d -> p t d", p=128)), [PEQ.last()])
    turn_gated(3)
    tables()
    tmpo = view(11264, 2, 2, 256)
    cnt = [0]

    def add_gated(u, p, b, pk):
        o = tmpo[:, cnt[0] % 2]
        cnt[0] += 1
        fr = tt(V, o, b, bc(grow[:, 256 * u:256 * u + 256].unsqueeze(1), 2, 256), ALU.mult, pk, gr)
        xs = x[:, 2 * p:2 * p + 2, 256 * u:256 * u + 256]
        tt(V, xs, xs, o, ALU.add, jx)
        return fr

    out_proj(oT, I["hg_w_out"][0], add_gated, mo, nxt)
    two_parts_end()
    barrier()

    xn_d = nc.dram_tensor("xn_d", (NTOK, F), f32, kind="Internal").ap()

    XN, H2T = view(4096, 4, F), view(8192, 8, 512)
    RT0 = 12288
    XG = [view(16384 + 1024 * i, F) for i in range(3)]
    XGT = [view(19456 + 1024 * i, 8, 128) for i in range(2)]
    SG = [view(21504 + 256 * i, 256) for i in range(2)]
    AA = [view(22016 + 256 * i, 256) for i in range(2)]
    AT = [view(22528 + 256 * i, 2, 128) for i in range(2)]
    YB = [view(23040 + 1024 * i, F) for i in range(2)]
    GROW, DIAG = view(25088, F), view(26112, F)
    SHA = view(27136, 4, 512)
    WR = view(29184, 8, 73)
    RTX = view(29768, 2048)
    RTY = view(31816, 64)

    def router_weights(layer, *w):
        NR = 16 if layer < 0 else 73
        o = wrt[:, 0:8 * NR].rearrange("p (k n) -> p k n", n=NR)
        if layer < 0:
            parts = ((o, I["router_w"]),)
        else:
            parts = ((o[:, :, 0:8], I["moe_group_w_2"][layer]), (o[:, :, 8:72], I["moe_expert_w_2"][layer]),
                     (o[:, :, 72:73], I["shared_gate_w_2"][layer]))
        return o, [LD.put(lambda e, o=o, s=s: e.dma_start(o, s.rearrange("(k p) n -> p k n", p=128),
                                                          allow_slow_non_contiguous=True), w) for o, s in parts]

    def moe(layer, NE, ab, wg, wu, wd, shared, gate_col, xn, after, router):
        G_ = 1 if layer < 0 else 2
        W, C, NTH, NOV = ((128, 128, 3, 7), (64, 40, 12, 26))[G_ - 1]
        NS, NV = NE // G_, NOV // G_
        NB, y_d = NS + NV, y_ds[NE]
        NY = (NE + NOV) * C
        th = thr[:, 16:16 + NTH] if G_ == 1 else thr[:, 0:NTH]
        NR = 16 if layer < 0 else 73
        rt = [RT0]

        def tmp(*shape, dt=None):
            n = 1
            for s in shape:
                n *= s
            o = view(rt[0], *shape)
            rt[0] += n
            assert rt[0] <= 14336
            return o if dt is None else o.bitcast(dt)

        wr, jw = router
        barrier()
        zx = [G(lambda e, o=o: e.memset(o, 0.0)) for o in XG][-1]
        xd = AD.put(lambda e: e.dma_start(xn_d.rearrange("(t p) d -> p t d", p=128), XN), [xn])
        bL = banks[7]

        def logits(k, j):
            mm(bL.ap[0:NR, :], wr[:, k, :], H2T[:, k, :], k == 0, k == 7, bL.free, j, *jw)

        transposed(XN, H2T, xn, ab=ab, turn=Banks(banks[0:6]), then=logits)
        LT = DIAG[0:NR, 0:512]
        pk_router = PEQ.last()
        bL.free = j = act(LT, bL.ap[0:NR, :], ACT.Copy, pk_router)
        b = banks[6]
        for t in range(4):
            o, i_ = b.ap[:, t * NR:(t + 1) * NR], LT[:, t * 128:(t + 1) * 128]
            PEQ.put(lambda e, o=o, i_=i_: e.transpose(o, i_, ident[0:NR, 0:NR]), [b.free, j], mark=None)
        pk = PEQ.last()
        gr = row_of(gate_col, GROW, RTX[:, 0:1024], pk)
        if layer < 0:
            gr = row_of(colD[:, 64:72], view(27136, F), RTX[:, 1024:2048])
        L = tmp(4, NR)
        b3 = b.ap[:, 0:4 * NR].rearrange("p (t n) -> p t n", n=NR)
        BIG = 1024.0

        def first_max(a, n, g, oh, mx, cand, mn=None):
            red(mx, a, ALU.max)
            tt(V, cand, a, bc(mx.unsqueeze(2), g, n), ALU.is_ge)
            stt(cand, cand, -BIG, bc(iota[:, 0:n].unsqueeze(1), g, n), ALU.mult, ALU.add)
            mn = RTY[:, 0:g] if mn is None else mn
            red(mn, cand, ALU.min)
            return tt(V, oh, cand, bc(mn.unsqueeze(2), g, n), ALU.is_equal)

        w12 = tmp(4, 2)
        m12 = [tmp(4), tmp(4)]
        oh1, oh2, el, cand = tmp(4, NE), tmp(4, NE), tmp(4, NE), tmp(4, NE)
        if layer < 0:
            j = act(L, b3, ACT.Exp, pk, scale=-1.0)
            b.free = j
            ts(V, L, L, 1.0, None, ALU.add, None, j)
            V(lambda e: e.reciprocal(L, L))
            tt(V, el, L, bc(ROWV["rb"].unsqueeze(1), 4, 16), ALU.add)
            e16 = el.rearrange("p t (g e) -> p (t g) e", e=4)
            o16, c16 = oh1.rearrange("p t (g e) -> p (t g) e", e=4), cand.rearrange("p t (g e) -> p (t g) e", e=4)
            t1, t2 = tmp(16), tmp(16)
            first_max(e16, 4, 16, o16, t1, c16)
            stt(c16, o16, -1e30, e16, ALU.mult, ALU.add)
            red(t2, c16, ALU.max)
            tt(V, t1, t1, t2, ALU.add)
            t3, mx4 = tmp(4, 4), tmp(4)
            first_max(t1.rearrange("p (t g) -> p t g", g=4), 4, 4, t3, mx4, t2.rearrange("p (t g) -> p t g", g=4))
            ng, eg, ohg = 4, 4, t3
        else:
            b.free = cp(V, L, b3, pk)
            gl, ohg, t3, mx4 = tmp(4, 8), tmp(4, 8), tmp(4, 8), tmp(4)
            tt(V, gl, L[:, :, 0:8], bc(ROWV[f"gb{layer}"].unsqueeze(1), 4, 8), ALU.add)
            tt(V, el, L[:, :, 8:72], bc(ROWV[f"eb{layer}"].unsqueeze(1), 4, 64), ALU.add)
            first_max(gl, 8, 4, ohg, mx4, t3)
            j = tt(V, gl, gl, bc(mx4.unsqueeze(2), 4, 8), ALU.subtract)
            j = act(gl, gl, ACT.Exp, j)
            psel = tmp(4)
            red(psel, gl, ALU.add, j)
            V(lambda e: e.reciprocal(psel, psel))
            sgate = tmp(4)
            j = act(sgate, L[:, :, 72], ACT.Exp, scale=-1.0)
            ts(V, sgate, sgate, 1.0, None, ALU.add, None, j)
            V(lambda e: e.reciprocal(sgate, sgate))
            ng, eg = 8, 8
        ts(V, ohg, ohg, -1.0, 1e30, ALU.add, ALU.mult)
        e32 = el.rearrange("p t (g e) -> p (t g) e", e=eg)
        tt(V, e32, e32, bc(ohg.rearrange("p t g -> p (t g)").unsqueeze(2), 4 * ng, eg), ALU.add)
        v1, v2 = tmp(4), tmp(4)
        first_max(el, NE, 4, oh1, v1, cand, m12[0])
        stt(el, oh1, -2e30, el, ALU.mult, ALU.add)
        first_max(el, NE, 4, oh2, v2, cand, m12[1])
        if layer < 0:
            for n, oh in enumerate((oh1, oh2)):
                tt(V, cand, oh, L, ALU.mult)
                red(w12[:, :, n], cand, ALU.add)
            tt(V, v1, w12[:, :, 0], w12[:, :, 1], ALU.add)
            V(lambda e: e.reciprocal(v1, v1))
            tt(V, w12, w12, bc(v1.unsqueeze(2), 4, 2), ALU.mult)
        else:
            j = tt(V, v2, v2, v1, ALU.subtract)
            j = act(v2, v2, ACT.Exp, j)
            ts(V, v1, v2, 1.0, None, ALU.add, None, j)
            V(lambda e: e.reciprocal(v1, v1))
            tt(V, w12[:, :, 0], v1, psel, ALU.mult)
            tt(V, w12[:, :, 1], w12[:, :, 0], v2, ALU.mult)
        M = el
        j = tt(V, M, oh1, oh2, ALU.add)
        b = allb.get()
        for t in range(5):
            o = b.ap[:, t * NE:(t + 1) * NE]
            for s in range(min(t, 3) + 1):
                mm(o, triS[:, :] if s == t else ones[:, :], M[:, s, :], s == 0, s == min(t, 3), j, b.free)
        pk = PEQ.last()
        nov, ove, ovs, cn = tmp(NE), tmp(NE), tmp(NE), tmp(NE)
        cp(V, cn, b.ap[:, 4 * NE:5 * NE], pk)
        big = RTX[:, 0:NE * NTH].rearrange("p (e n) -> p e n", n=NTH)
        tt(V, big, bc(cn.unsqueeze(2), NE, NTH), bc(th.unsqueeze(1), NE, NTH), ALU.is_gt)
        red(nov, big, ALU.add)
        V(lambda e: e.tensor_tensor_scan(ove, ones[:, 0:NE], nov, 0.0, ALU.mult, ALU.add))
        tt(V, ovs, ove, nov, ALU.subtract)
        pp, ee, oo, bb, ff, hh = (tmp(4, 2) for _ in range(6))
        pos3 = b.ap[:, 0:4 * NE].rearrange("p (t n) -> p t n", n=NE)
        for n, oh in enumerate((oh1, oh2)):
            tt(V, cand, oh, pos3, ALU.mult)
            red(pp[:, :, n], cand, ALU.add)
            ts(V, ee[:, :, n], m12[n], BIG, None, ALU.add, None)
            tt(V, cand, oh, bc(ovs.unsqueeze(1), 4, NE), ALU.mult)
            red(oo[:, :, n], cand, ALU.add)
        b.free = VEQ.last()
        f8 = lambda a: a.rearrange("p t n -> p (t n)")
        big = RTX[:, 0:8 * NTH].rearrange("p (e n) -> p e n", n=NTH)
        tt(V, big, bc(f8(pp).unsqueeze(2), 8, NTH), bc(th.unsqueeze(1), 8, NTH), ALU.is_ge)
        red(f8(bb), big, ALU.add)
        stt(pp, bb, -float(C), pp, ALU.mult, ALU.add)
        ts(V, ff, bb, 1.0, None, ALU.min, None)
        stt(oo, bb, float(NE - 1), oo, ALU.add, ALU.add)
        tt(V, oo, oo, ee, ALU.subtract)
        tt(V, oo, oo, ff, ALU.mult)
        tt(V, ee, ee, oo, ALU.add)
        yi = tmp(4, 2, dt=i32)
        stt(yi, ee, float(C), pp, ALU.mult, ALU.add)
        if G_ == 2:
            hi = hh.bitcast(i32)
            cp(V, hi, ee)
            V(lambda e: e.tensor_single_scalar(hi, hi, 1, ALU.bitwise_and))
            cp(V, ff, hi)
            tt(V, ee, ee, ff, ALU.subtract)
            ts(V, ee, ee, 0.5, None, ALU.mult, None)
            stt(pp, ff, float(C), pp, ALU.mult, ALU.add)
        ohb = RTX[:, 0:8 * NB].rearrange("p (t n k) -> p t n k", n=2, k=NB)
        ohp = RTX[:, 8 * NB:8 * NB + 1024].rearrange("p (t n k) -> p t n k", n=2, k=128)
        ob3, op3 = ohb.rearrange("p t n k -> p (t n) k"), ohp.rearrange("p t n k -> p (t n) k")
        tt(V, ob3, bc(iota[:, 0:NB].unsqueeze(1), 8, NB), bc(f8(ee).unsqueeze(2), 8, NB), ALU.is_equal)
        o4 = RTX[:, 0:8 * NB].rearrange("p (t n) -> p t n", t=4)
        tt(V, o4, o4, bc(tok1[:, :].unsqueeze(2), 4, 2 * NB), ALU.mult)
        j = tt(V, op3, bc(iota[:, :].unsqueeze(1), 8, 128), bc(f8(pp).unsqueeze(2), 8, 128), ALU.is_equal)
        b = allb.get()
        for n in range(8):
            mm(b.ap[:, 0:NB], op3[:, n, :], ob3[:, n, :], n == 0, n == 7, j, b.free)
        pk = PEQ.last()
        tk, tz = tmp(NB), tmp(NB)
        idx = tmp(NB, dt=i32)
        cp(V, tk, b.ap[:, 0:NB], pk)
        b.free = VEQ.last()
        ts(V, tz, tk, 0.0, 5000.0, ALU.is_equal, ALU.mult)
        idx_done = stt(idx, tk, -1.0, tz, ALU.add, ALU.add)
        def shared_steps():
            sgw, suw, sdw = shared
            u0 = Unit()
            u0.done = ei_done
            RS = Ring([8, 9], {8: u0, 9: u0})
            pair = [RS.cols(sgw, 0), RS.cols(suw, 0)]
            yield
            for p in range(2):
                ug, uu = pair
                for f in range(2):
                    o = SHA[:, 2 * p + f, :]
                    for un in pair:
                        b = allb.get()
                        for k in range(8):
                            mm(b.ap, un.ap[:, k, f * 128:(f + 1) * 128], H2T[:, k, :], k == 0, k == 7, un.ready, b.free)
                        un.done = pk = PEQ.last()
                        if un is ug:
                            b.free = act(o, b.ap, ACT.Silu, pk)
                        else:
                            b.free = sh = tt(V, o, o, b.ap, ALU.mult, pk, ACQ.last())
                        yield
                yield
                if p == 0:
                    pair = [RS.cols(sgw, 256), RS.cols(suw, 256)]
                else:
                    dn = [RS.load(sdw[256 * i:256 * i + 256, :].rearrange("(k p) n -> p k n", p=128), 2) for i in range(2)]
                yield
            for t in range(4):
                for n in range(2):
                    b = allb.get()
                    for k in range(4):
                        un = dn[k // 2]
                        mm(b.ap, SHA[:, k, t * 128:(t + 1) * 128], un.ap[:, k % 2, n * 512:(n + 1) * 512],
                           k == 0, k == 3, un.ready, b.free, sh)
                    pk = PEQ.last()
                    o = XN[:, t, n * 512:(n + 1) * 512]
                    b.free = ts(V, o, b.ap, sgate[:, t:t + 1], None, ALU.mult, None, pk, xd)
                    yield

        free = dict(xg=[zx] * 3, xgt=[zx] * 2, at=[zx] * 2, yb=[None] * 2, sg=[zx] * 2, aa=[zx] * 2)
        gath, st = {}, {}

        OD = Dma(f"d_ov{layer + 1}_", GPQ, NV, once=True)

        def gather(n):
            i = n % 3
            gath[n] = (GD if n < NS else OD).put(lambda e: e.indirect_dma_start(
                out=XG[i][0:G_ * C], out_offset=None, in_=xn_d,
                in_offset=bass.IndirectOffsetOnAxis(ap=idx[0:G_ * C, n:n + 1], axis=0),
                bounds_check=NTOK - 1, oob_is_err=False), [idx_done, xd, free["xg"][i]])

        def turn(n):
            i = n % 2
            ba, bb = allb.get(), allb.get()
            for k in range(8):
                b = (ba, bb)[k // 4]
                tr(b.ap[:, (k % 4) * 128:(k % 4) * 128 + 128], XG[n % 3][:, k * 128:(k + 1) * 128], b.free, gath[n])
            pk = PEQ.last()
            free["xg"][n % 3] = pk
            for k in range(4):
                ba.free = ts(V, XGT[i][:, k, :], ba.ap[:, k * 128:(k + 1) * 128], ab[:, k:k + 1], ab[:, 8 + k:9 + k],
                             ALU.mult, ALU.add, pk, free["xgt"][i])
            for k in range(4, 8):
                bb.free = act(XGT[i][:, k, :], bb.ap[:, (k - 4) * 128:(k - 3) * 128], ACT.Identity, pk, free["xgt"][i],
                              scale=ab[:, k:k + 1], bias=ab[:, 8 + k:9 + k])
            st[n] = (ba.free, bb.free)

        regs, count = {}, {}

        def unit_srcs(n):
            out_ = []
            for u in range(G_ * n, G_ * n + G_):
                if u < NE:
                    srcs = [w[u].rearrange("(k p) n -> p k n", p=128) for w in (wg, wu, wd)]
                else:
                    jj = u - NE

                    def dyn(w, key, jj=jj):
                        def src(e):
                            if key == 0:
                                regs[jj] = e.value_load(eii[0:1, jj:jj + 1], min_val=0, max_val=NE - 1)
                            return w[bass.ds(regs[jj], 1)].rearrange("a (k p) n -> p (a k) n", p=128)
                        return src
                    srcs = [dyn(wg, 0), dyn(wu, 1), dyn(wd, 2)]
                out_.append(srcs)
            return out_

        units = {}

        def loads(n, ws):
            srcs = unit_srcs(n)
            for w in ws:
                units[n, w] = [R.load(srcs[h][w], (8, 8, 2)[w]) for h in range(G_)]

        hs2 = [slice(W * h, W * h + W) for h in range(G_)]
        aas = {}

        def gate_up(n):
            i = n % 2
            gu = units[n, 0], units[n, 1]
            bg, bu = allb.get(), allb.get()
            for w, b in enumerate((bg, bu)):
                for k in range(8):
                    for h in range(G_):
                        mm(b.ap[hs2[h], 0:256], XGT[i][:, k, C * h:C * h + W], gu[w][h].ap[:, k, :],
                           k == 0, k == 7, gu[w][h].ready, b.free, *st[n])
                for h in range(G_):
                    gu[w][h].done = PEQ.last()
            free["xgt"][i] = pk = PEQ.last()
            bg.free = s = act(SG[i], bg.ap[:, 0:256], ACT.Silu, gu[0][0].done, free["sg"][i])
            bu.free = aas[n] = free["sg"][i] = tt(V, AA[i], SG[i], bu.ap[:, 0:256], ALU.mult, pk, s, free["aa"][i])

        def hidden(n):
            i = n % 2
            b = allb.get()
            for f in range(2):
                tr(b.ap[:, f * 128:(f + 1) * 128], AA[i][:, f * 128:(f + 1) * 128], aas[n], b.free)
            free["aa"][i] = pk = PEQ.last()
            b.free = aas[n] = cp(V, AT[i], b.ap[:, 0:256].rearrange("p (f s) -> p f s", s=128), pk, free["at"][i])

        def down(n):
            i = n % 2
            dd = units[n, 2]
            bn = [allb.get(), allb.get()]
            for f in range(2):
                b = bn[f]
                for k in range(2):
                    for h in range(G_):
                        mm(b.ap[hs2[h], :], AT[i][:, k, hs2[h]], dd[h].ap[:, k, f * 512:(f + 1) * 512],
                           k == 0, k == 1, dd[h].ready, b.free, aas[n])
                PEQ.last()
            pk = PEQ.last()
            for h in range(G_):
                dd[h].done = pk
            free["at"][i] = pk
            before = free["yb"][i] or []
            bn[0].free = e0 = cp(V, YB[i][:, 0:512], bn[0].ap, pk, *before)
            bn[1].free = e1 = act(YB[i][:, 512:1024], bn[1].ap, ACT.Copy, pk, *before)
            free["yb"][i] = [AD.put(lambda e, h=h: e.dma_start(
                y_d[(G_ * n + h) * C:(G_ * n + h + 1) * C, :], YB[i][W * h:W * h + C, :]), [e0, e1]) for h in range(G_)]

        for n in range(3):
            gather(n)
        loads(0, (0, 1))
        loads(1, (0, 1))
        turn(0)
        ei = tmp(NOV)
        eii = tmp(NOV, dt=i32)
        big = RTX[:, 0:NOV * NE].rearrange("p (j e) -> p j e", e=NE)
        tt(V, big, bc(ove.unsqueeze(1), NOV, NE), bc(iota[:, 0:NOV].unsqueeze(2), NOV, NE), ALU.is_le)
        red(ei, big, ALU.add)
        ts(V, eii, ei, float(NE - 1), None, ALU.min, None)
        nvi = tmp(1, dt=i32)
        ei_done = cp(V, nvi, ove[:, NE - 1:NE])
        S = shared_steps() if shared is not None else iter(())
        next(S, None)
        for n in range(NS):
            gate_up(n)
            if n:
                hidden(n - 1)
            if n + 3 < NS:
                gather(n + 3)
            if n + 1 < NS:
                turn(n + 1)
            if n:
                loads(n - 1, (2,))
                down(n - 1)
            if 0 < n < NS - 1:
                loads(n + 1, (0, 1))
            next(S, None)
            if n == 4 and layer < 1:
                ahead.append(router_weights(layer + 1, pk_router))
        hidden(NS - 1)
        for _ in S:
            pass
        loads(NS - 1, (2,))
        down(NS - 1)
        barrier()

        def fetch(e):
            count[e] = e.value_load(nvi[0:1, 0:1], min_val=0, max_val=NOV)

        for q in QS:
            q.put(fetch, [ei_done], mark=False)
        for q in QS:
            q.begin()
        for j in range(NV):
            for q in QS:
                q.begin()
            gather(NS + j)
            loads(NS + j, (0, 1, 2))
            turn(NS + j)
            gate_up(NS + j)
            hidden(NS + j)
            down(NS + j)
            for q in QS:
                q.end(lambda e, j=j: count[e] > G_ * j)
        for q in QS:
            q.end(lambda e: count[e] > 0)
        tables()
        done = barrier()
        ybuf = [view(o + 1024 * i, F) for o in (8192, 16384) for i in range(4)]
        gm = [GD.put(lambda e, i=i: e.indirect_dma_start(
            out=ybuf[i], out_offset=None, in_=y_d, in_offset=bass.IndirectOffsetOnAxis(ap=yi[:, i // 2, i % 2:i % 2 + 1], axis=0),
            bounds_check=NY - 1, oob_is_err=False), done) for i in range(8)]
        SPQ.first = SPQ.first + [gm[7]]
        a0s = [act(XN[:, t, :], ybuf[2 * t], ACT.Copy, gm[2 * t], scale=w12[:, t, 0:1])
               for t in range(4 if shared is None else 0)]

        def mix(t):
            if shared is None:
                a0 = a0s[t]
            else:
                stt(XN[:, t, :], ybuf[2 * t], w12[:, t, 0:1], XN[:, t, :], ALU.mult, ALU.add, gm[2 * t])
            j = stt(XN[:, t, :], ybuf[2 * t + 1], w12[:, t, 1:2], XN[:, t, :], ALU.mult, ALU.add, gm[2 * t + 1], *([a0] if shared is None else []))
            if layer < 0:
                tt(V, XN[:, t, :], XN[:, t, :], GROW, ALU.mult, gr)
                j = tt(V, x[:, t, :], x[:, t, :], XN[:, t, :], ALU.add)
                return square(t, x[:, t, :], 0, j)
            return square(t, XN[:, t, :], 0, j)

        def final(t, r):
            return stt(x[:, t, :], x[:, t, :], rs[:, t:t + 1], view(27136, F), ALU.mult, ALU.mult, r, gr)

        def stored(t, r):
            j = last_(t, r)
            AD.put(lambda e: e.dma_start(out[0, t * 128:(t + 1) * 128, :], x[:, t, :]), [j])

        last_ = post(GROW, gr)
        return tiles(mix, final if layer < 0 else last_ if after else stored, after)

    def square(t, src, c, *w):
        ss = rs[:, c + t:c + t + 1]
        act(DIAG, src, ACT.Square, *w, accum_out=ss)
        return rsqrt(ss, F)

    def post(grow, gr, *w):
        def f(t, r):
            stt(XN[:, t, :], XN[:, t, :], rs[:, t:t + 1], grow, ALU.mult, ALU.mult, r, gr)
            return tt(V, x[:, t, :], x[:, t, :], XN[:, t, :], ALU.add, *w)
        return f

    def norm_x(t, r):
        return act(XN[:, t, :], x[:, t, :], ACT.Copy, r, scale=rs[:, 4 + t:5 + t])

    def tiles(first, second, after):
        m, j = {}, None
        for i in range(4 + 2):
            if i < 4:
                m[i] = first(i)
            if 0 <= i - 1 < 4:
                j = second(i - 1, m[i - 1])
                if after:
                    m[i - 1] = after(i - 1, j)
            if after and 0 <= i - 2 < 4:
                j = norm_x(i - 2, m[i - 2])
        return j

    def again(t, j):
        return square(t, x[:, t, :], 4, j)

    def x_tile(t):
        return square(t, x[:, t, :], 4, VEQ.last())

    for t in range(4):
        xn = norm_x(t, x_tile(t))
    ahead = [router_weights(-1)]
    xn = moe(-1, 16, ABS1[:, 32:48], I["moe_w_gate"][0], I["moe_w_up"][0], I["moe_w_down"][0], None, m1[:, 40:48, 0], xn, again, ahead[-1])

    two_parts_begin()
    hc2 = part(18432), part(27136)
    wc = I["conv_in_w_2"][0]
    nxt = two_parts(R.cols(wc, F))
    h0 = transposed2(XN, hc2, xn, ab=abn[0][0], full=H2T)
    YT = view(12288, 8, 512)
    y2 = part(8192), part(12288)
    CG = [view(16384 + 512 * i, 512) for i in range(2)]
    U = [view(17408 + 512 * i, 512) for i in range(2)]
    cw = lambda i, f: colB[:, 96 + 8 * i + f:97 + 8 * i + f]
    yj = []
    todo = [(p, s) for p in range(4) for s in (1, 2, 0)]
    cols_of = lambda n: R.cols(wc, F * todo[n][1] + 256 * todo[n][0])
    jcg, ju = [None] * 2, [h0[7][1]] * 2
    for n, (p, s) in enumerate(todo):
        i, wp, jw = nxt
        if n + 1 < len(todo):
            nxt = two_parts(cols_of(n + 1))
        bs = [allb.get(), allb.get()]
        for f, b in enumerate(bs):
            c = slice(f * 128, (f + 1) * 128)
            for k in range(8):
                mm3(b.ap, (wp[0][:, k, c], wp[1][:, k, c]), (hc2[0][:, k, :], hc2[1][:, k, :]), k == 0, k == 7,
                    b.free, *jw, *h0[k])
            pk = PEQ.last()
            if f:
                wread[i] = [pk]
            ft = 2 * p + f
            u, y = U[f], YT[:, ft, :]
            if s == 1:
                jcg[f] = b.free = act(CG[f], b.ap, ACT.Copy, pk, ju[f])
            elif s == 2:
                ju[f] = b.free = tt(V, u, CG[f], b.ap, ALU.mult, pk, jcg[f])
                ts(V, y, u, cw(2, ft), None, ALU.mult, None)
                stt(y[:, 1:512], u[:, 0:511], cw(1, ft), y[:, 1:512], ALU.mult, ALU.add)
                stt(y[:, 2:512], u[:, 0:510], cw(0, ft), y[:, 2:512], ALU.mult, ALU.add)
            else:
                b.free = j = tt(V, y, y, b.ap, ALU.mult, pk)
                jh = act(y2[0][:, ft, :], y, ACT.Copy, j, h0[7][1])
                yj.append((jh, tt(V, y2[1][:, ft, :], y, y2[0][:, ft, :].bitcast(f32), ALU.subtract, jh)))
    gr = row_of(gts[0][0], GROW, DIAG)

    def keep_rows(u, p, b, pk):
        o = XN[:, 2 * p:2 * p + 2, 256 * u:256 * u + 256]
        return act(o, b, ACT.Copy, pk) if p else cp(V, o, b, pk)

    out_proj(y2, I["conv_out_w_2"][0], keep_rows, yj)
    two_parts_end()
    xn = tiles(lambda t: square(t, XN[:, t, :], 0, VEQ.last()), post(GROW, gr), again)

    def moe2(i, xn, after):
        return moe(i, 64, abn[i][1], I["moe_w_gate_2"][i], I["moe_w_up_2"][i], I["moe_w_down_2"][i],
            (I["shared_w_gate_2"][i], I["shared_w_up_2"][i], I["shared_w_down_2"][i]), gts[i][1], xn, after, ahead[-1])

    xn = moe2(0, xn, again)

    x_d = nc.dram_tensor("x_d", (NTOK, F), f32, kind="Internal").ap()
    xs = AD.put(lambda e: e.dma_start(x_d.rearrange("(t p) d -> p t d", p=128), x), [VEQ.last()])
    hG = H2T
    hg_done = transposed(XN, hG, xn, ab=abn[1][0])
    barrier()
    wi = I["gdn_in_w_2"][0]
    z = view(0, 4, F)
    WBA = view(28672, 8, 16)
    jb = LD.put(lambda e: e.dma_start(WBA, wi[:, 4096:4112].rearrange("(k p) n -> p k n", p=128)), barrier())
    Uu = view(4096, 4, F)
    nwT = view(12288, 8, 512)
    qdT = view(16384, 8, 512)
    kde = view(20480, 4, F)
    atT = view(24576, 8, 256)
    tail = [28800]

    def tl(*shape):
        n = 1
        for s in shape:
            n *= s
        o = view(tail[0], *shape)
        tail[0] += n
        assert tail[0] <= 32256
        return o

    b = allb.get()
    for t in range(4):
        for k in range(8):
            mm(b.ap[:, t * 16:(t + 1) * 16], hG[:, k, t * 128:(t + 1) * 128], WBA[:, k, :], k == 0, k == 7, b.free, jb)
    pk = PEQ.last()
    ba = tl(4, 16)
    b.free = cp(V, ba, b.ap[:, 0:64].rearrange("p (t n) -> p t n", n=16), pk)
    beta, gg, g1, gc, gk, egc = (tl(4, 8) for _ in range(6))
    j = act(beta, ba[:, :, 0:8], ACT.Exp, b.free, scale=-1.0)
    ts(V, beta, beta, 1.0, None, ALU.add, None, j)
    V(lambda e: e.reciprocal(beta, beta))
    j = tt(V, gg, ba[:, :, 8:16], bc(ROWV["dt"].unsqueeze(1), 4, 8), ALU.add)
    act(g1, gg, ACT.Abs, j)
    act(g1, g1, ACT.Exp, scale=-1.0)
    j = act(g1, g1, ACT.Ln, bias=ones[:, 0:1])
    ts(V, gg, gg, 0.0, None, ALU.max, None, j)
    tt(V, gg, gg, g1, ALU.add, j)
    ea = tl(8)
    j = act(ea, ROWV["alog"], ACT.Exp)
    ts(V, ea, ea, -1.0, None, ALU.mult, None, j)
    j = tt(V, gg, gg, bc(ea.unsqueeze(1), 4, 8), ALU.mult)
    b = allb.get()
    g32 = gg.rearrange("p t h -> p (t h)")
    mm(b.ap[:, 0:32], mf[:, :], g32, True, True, j, b.free)
    mm(b.ap[:, 32:64], b64[:, :], g32, True, True)
    pk = PEQ.last()
    cp(V, gc.rearrange("p t h -> p (t h)"), b.ap[:, 0:32], pk)
    b.free = j = tt(V, gk.rearrange("p t h -> p (t h)"), b.ap[:, 32:64], gc.rearrange("p t h -> p (t h)"), ALU.subtract)
    act(gk, gk, ACT.Exp, j)
    j = act(egc, gc, ACT.Exp)
    tt(V, egc, egc, beta, ALU.mult, j)
    decs = tl(8, 8)
    bar = barrier()
    R.slots, R.n = [0, 1, 2, 3], 0
    tq = [0]

    def rtl(*shape):
        n = 1
        for s in shape:
            n *= s
        v_ = ring[:, 8192 + tq[0]:8192 + tq[0] + n]
        tq[0] += n
        assert tq[0] <= 8192
        if len(shape) == 1:
            return v_
        return v_.rearrange("p (a b) -> p a b", a=shape[0])

    held = [R.held[s] for s in (4, 5, 6, 7)]
    freed = [lambda u=u: u.done for u in held]
    for q in (VEQ, ACQ, GPQ):
        q.first = q.first + freed
    Ts = [[rtl(512) for _ in range(3)] for _ in range(2)]
    XP = rtl(512)
    bv, bk = rtl(4, 128), rtl(4, 128)
    DC, DS, NN, NT, P2, PT, P4, XQ, XX, MM, YY = (rtl(4, 64) for _ in range(11))
    DCs = [rtl(4, 64) for _ in range(2)]
    GR = tl(512)
    RR = tl(512)
    gcw = lambda i, f: colC[:, 24 * i + f:24 * i + f + 1]
    gdu = {}
    HV = (slice(0, 64), slice(64, 128))
    b3 = lambda b: b.ap.rearrange("p (t c) -> p t c", c=128)
    c3 = lambda b: b.ap[:, 0:256].rearrange("p (t c) -> p t c", c=64)
    m3 = lambda m: bc(m[:, :].unsqueeze(1), 4, 64)
    pbk, nbk, sbk = Banks(banks[0:2]), Banks(banks[2:3]), Banks(banks[3:8])
    H_ = {}


    def pre(h):
        if h % 2 == 0:
            for s in range(3):
                gdu[s] = R.cols(wi, F * s + 128 * h)
        off = 128 * (h % 2)
        conv, taps = [], []

        def tap(b, dst, ft, pk):
            j = act(dst, b.ap, ACT.Copy, pk, *H_.get(("read", h - 2), []), scale=gcw(3, ft))
            yield
            for i in (2, 1, 0):
                w = 3 - i
                j = stt(dst[:, w:512], b.ap[:, 0:512 - w], gcw(i, ft), dst[:, w:512], ALU.mult, ALU.add, j)
                if i:
                    yield
            b.free = j
            conv.append(j)

        for s, dst in enumerate(Ts[h % 2]):
            un, ft = gdu[s], 8 * s + h
            b = pbk.get()
            for k in range(8):
                mm(b.ap, un.ap[:, k, off:off + 128], hG[:, k, :], k == 0, k == 7, un.ready, b.free)
                if k % 2:
                    un.done = pk = PEQ.last()
                    for g in taps[-1:]:
                        next(g, None)
                    yield
            taps.append(tap(b, dst, ft, pk))
            next(taps[-1])
        for _ in range(4):
            for g in taps:
                next(g, None)
        H_["conv", h] = conv
        yield

    def norm(h):
        DX = DCs[h % 2]
        j = tt(G, XP.rearrange("p (t c) -> p t c", c=128), bc(mf[:, :].unsqueeze(1), 4, 128), bc(gg[:, :, h:h + 1], 4, 128), ALU.mult,
               H_.get(("bc", h - 1), bar[0]), *bar)
        yield
        b = nbk.get()
        mm(b.ap, ones[:, :], XP, True, True, j, b.free)
        H_["bc", h] = pk = PEQ.last()
        for n, hv in enumerate(HV):
            tt(V, DX[hv], bc(gc[hv, :, h:h + 1], 4, 64), b3(b)[hv, :, 64 * n:64 * n + 64], ALU.subtract, pk, *bar)
        j = ts(V, DX, DX, 0.0, None, ALU.min, None)
        yield
        b.free = act(qdT[:, h, :], b.ap, ACT.Exp, j)
        H_["decay", h] = act(DX, DX, ACT.Exp)
        made = [act(dst, dst, ACT.Silu, j) for dst, j in zip(Ts[h % 2], H_["conv", h])]
        tables()
        for n, (sc_, eb) in enumerate(((128.0, 1), (1.0, 0))):
            dst = Ts[h % 2][n]
            j = act(RR, dst, ACT.Square)
            for _ in range(2 - n):
                yield
            b = nbk.get()
            mm(b.ap, ones[:, :], RR, True, True, j, b.free)
            pk = PEQ.last()
            yield
            b.free = act(GR, b.ap, ACT.Ln, pk, GPQ.last(), scale=sc_, bias=epsc[:, eb:eb + 1])
            je = act(GR, GR, ACT.Exp, scale=-0.5)
            made[n] = tt(G, dst, dst, GR, ALU.mult, je)
        H_["made", h] = made
        yield

    def quads(b, l, r_, *w):
        for t in range(4):
            for hv in HV:
                mm(b.ap[hv, t * 64:(t + 1) * 64], l[hv, t, :], r_[hv, t, :], True, True, b.free, *w)
        return PEQ.last()

    def turned(src, dst, *w):
        b = sbk.get()
        for t in range(4):
            for hv in HV:
                mm(b.ap[hv, t * 64:(t + 1) * 64], src[hv, t, :], ident[hv, hv], True, True, b.free, *w)
        pk = PEQ.last()
        b.free = cp(V, dst, c3(b), pk)
        return b.free

    def sol(h):
        hc = slice(128 * h, 128 * h + 128)
        TQ, TK, TV = Ts[h % 2]
        DX, je = DCs[h % 2], H_["decay", h]
        mq, mk, mv = H_["made", h]
        end = H_.get(("end", h - 1), bar[0])
        cp(V, decs[:, h, :], qdT[:, h, 63:512:64], je)
        jq = tt(G, qdT[:, h, :], qdT[:, h, :], TQ, ALU.mult, VEQ.last(), mq)
        bq, bk2 = sbk.get(), sbk.get()
        for b, l in ((bk2, TK), (bq, TQ)):
            for t in range(4):
                for n, hv in enumerate(HV):
                    c = slice(t * 128 + 64 * n, t * 128 + 64 * n + 64)
                    mm(b.ap[hv, t * 64:(t + 1) * 64], l[:, c], TK[:, c], True, True, mq, mk, b.free)
            PEQ.last()
        ps_ = PEQ.last()
        tt(V, DX, DX, m3(mbc), ALU.mult, je)
        tt(V, DS, DX, m3(mbsc), ALU.mult)
        tt(V, DS, DS, bc(beta[:, :, h:h + 1], 4, 64), ALU.mult)
        yield
        bk2.free = jn = tt(V, NN, c3(bk2), DS, ALU.mult, ps_)
        bq.free = j = tt(V, XQ, c3(bq), DX, ALU.mult)
        jt = turned(NN, NT, jn)
        bvr, bkr = sbk.get(), sbk.get()
        for b, src in ((bvr, TV), (bkr, TK)):
            for t in range(4):
                tr(b.ap[:, t * 128:(t + 1) * 128], src[:, t * 128:(t + 1) * 128], mv, b.free)
        pk = PEQ.last()
        H_["read", h] = [pk, jq]
        jd = tt(V, DC, NN, m3(levc[0]), ALU.mult, end)
        yield
        jdt = tt(V, PT, NT, m3(levc[0]), ALU.mult, jt)
        b, b2 = sbk.get(), sbk.get()
        p1 = quads(b, PT, DC, jd, jdt)
        b.free = j2 = cp(V, P2, c3(b), p1)
        p2 = quads(b2, DC, PT)
        yield
        b2.free = j2t = cp(V, NT, c3(b2), p2)
        tt(V, XX, NT, m3(idc), ALU.add, end)
        b = sbk.get()
        p1 = quads(b, P2, NT, j2, j2t)
        j4 = p1
        bP4 = b
        bvr.free = tt(V, bv, b3(bvr), bc(beta[:, :, h:h + 1], 4, 128), ALU.mult, pk, end)
        yield
        j4 = cp(V, P4, c3(bP4), j4)
        bP4.free = tt(V, XX, XX, P4, ALU.add)
        b = sbk.get()
        p1 = quads(b, P2, P4, j4)
        tt(V, bk, b3(bkr), bc(egc[:, :, h:h + 1], 4, 128), ALU.mult, pk)
        yield
        b.free = jx = tt(V, XX, XX, c3(b), ALU.add, p1)
        bkr.free = rv = tt(V, kde[:, :, hc], b3(bkr), bc(gk[:, :, h:h + 1], 4, 128), ALU.mult)
        b = sbk.get()
        p1 = quads(b, DC, XX, jx)
        yield
        b.free = jm = tt(V, XX, XX, c3(b), ALU.subtract, p1)
        for i in (1, 2, 3):
            jmt = turned(XX, MM, jm)
            jl = tt(V, DC, NN, m3(levc[i]), ALU.mult)
            b = sbk.get()
            p1 = quads(b, DC, XX, jl)
            b.free = jy = cp(V, YY, c3(b), p1)
            yield
            b = sbk.get()
            p1 = quads(b, MM, YY, jmt, jy)
            if i == 1:
                turned(XQ, atT[:, h, :].rearrange("p (t c) -> p t c", c=64), j)
            yield
            b.free = jm = tt(V, XX, XX, c3(b), ALU.subtract, p1)
        b, b0, b1 = (sbk.get() for _ in range(3))
        for t in range(4):
            for hv in HV:
                mm(b.ap[hv, t * 128:(t + 1) * 128], XX[hv, t, :], bv[hv, t, :], True, True, jm, rv, b.free)
        pk = PEQ.last()
        b.free = act(Uu[:, :, hc], b3(b), ACT.Copy, pk)
        n4 = nwT[:, h, :].rearrange("p (t n c) -> p t n c", n=2, c=64)
        for n, b in enumerate((b0, b1)):
            for t in range(4):
                mm(b.ap[:, t * 64:(t + 1) * 64], bk[HV[n], t, :], XX[HV[n], t, :], True, True, b.free)
            pk = PEQ.last()
            b.free = act(n4[:, :, n, :], c3(b), ACT.Copy, pk, scale=-1.0)
        H_["end", h] = pk
        yield

    def gates():
        for u in range(4):
            un = R.cols(wi, 3 * F + 256 * u)
            for p in range(2):
                b = pbk.get()
                for t in (2 * p, 2 * p + 1):
                    for k in range(8):
                        mm(b.ap[:, (t % 2) * 256:(t % 2) * 256 + 256], hG[:, k, t * 128:(t + 1) * 128],
                           un.ap[:, k, :], k == 0, k == 7, un.ready, b.free)
                        if k % 4 == 3:
                            un.done = pk = PEQ.last()
                            if k == 3 or t % 2 == 0:
                                yield
                o = z[:, 2 * p:2 * p + 2, 256 * u:256 * u + 256]
                b.free = act(o, b.ap.rearrange("p (t n) -> p t n", t=2), ACT.Silu, pk)
                yield
        for t in range(4):
            o = z[:, t, :].rearrange("p (h d) -> p h d", d=128)
            tt(G, o, o, bc(ROWV["gdn_norm"].unsqueeze(1), 8, 128), ALU.mult, ACQ.last())
        tables()

    for _ in pre(0):
        pass
    N, P = norm(0), pre(1)
    for _ in P:
        next(N, None)
    for _ in N:
        pass
    Z = gates()
    for h in range(8):
        N = norm(h + 1) if h < 7 else iter(())
        P = pre(h + 2) if h < 6 else Z
        for _ in sol(h):
            next(N, None)
            next(P, None)
        for g in (N, P if h != 6 else ()):
            for _ in g:
                pass
    barrier()
    oR = view(8192, 4, F)
    first = R.cols(I["gdn_out_w_2"][0], 0)
    Sp = [ring[:, 8192 + 1024 * i:9216 + 1024 * i] for i in range(2)]
    Sd, vn, sq = (ring[:, 10240 + 1024 * i:11264 + 1024 * i] for i in range(3))
    s3 = lambda a: a.rearrange("p (h d) -> p h d", d=128)
    js = [fill(Sp[0], 0.0)] * 2
    hh_ = [slice(0, 512), slice(512, 1024)]
    hd = lambda h: slice(128 * h, 128 * h + 128)
    fr = {}
    po = {}
    jz = None

    def read_out(p, Q, Q2):
        j = act(sq, oR[:, p, :], ACT.Square, VEQ.last())
        red(hs[:, p, :], s3(sq), ALU.add, j)
        j = rsqrt(hs[:, p, :], 128, VEQ.last())
        tt(Q, s3(oR[:, p, :]), s3(oR[:, p, :]), bc(hs[:, p, :].unsqueeze(2), 8, 128), ALU.mult, j)
        return tt(Q2, oR[:, p, :], oR[:, p, :], z[:, p, :], ALU.mult)

    for n in range(8):
        p, off = n // 2, 64 * (n % 2)
        half = slice(off, off + 64)
        cs = slice(64 * n, 64 * n + 64)
        Sn, Sx = Sp[n % 2], Sp[(n + 1) % 2]
        A_ = [PS[:, (0, 6)[n % 2] + f, :] for f in range(2)]
        B_ = [PS[:, 4 + f, :] for f in range(2)]
        C_ = [PS[:, 2 + f, :] for f in range(2)]
        pa, jn, pb_ = [0, 0], [0, 0], [0, 0]
        loc = lambda h: slice(128 * (h % 4), 128 * (h % 4) + 128)
        for f in range(2):
            for h in range(4 * f, 4 * f + 4):
                mm(A_[f][half, loc(h)], nwT[:, h, cs], Sn[:, hd(h)], True, True, js[f], *fr.get(("A", n % 2, f), []))
            pa[f] = PEQ.last()
        jsd = [tt(G, s3(Sd[:, hh_[f]]), s3(Sn[:, hh_[f]]), bc(decs[:, 4 * f:4 * f + 4, n:n + 1], 4, 128), ALU.mult, js[f])
               for f in range(2)]
        for f in range(2):
            jn[f] = tt(V, vn[half, hh_[f]], A_[f][half, :], Uu[half, p, hh_[f]], ALU.add, pa[f], *po.get((n - 2, f), []))
            fr["A", n % 2, f] = [jn[f]]
            for h in range(4 * f, 4 * f + 4):
                mm(B_[f][:, loc(h)], kde[half, p, hd(h)], vn[half, hd(h)], True, True, jn[f], *fr.get(("B", f), []))
            pb_[f] = PEQ.last()
        for f in range(2):
            js[f] = tt(V, Sx[:, hh_[f]], Sd[:, hh_[f]], B_[f], ALU.add, pb_[f], jsd[f], *po.get((n - 1, f), []))
            fr["B", f] = [js[f]]
            for h in range(4 * f, 4 * f + 4):
                mm(C_[f][half, loc(h)], qdT[:, h, cs], Sn[:, hd(h)], True, False, *fr.get(("C", f), []))
                mm(C_[f][half, loc(h)], atT[half, h, p * 64:(p + 1) * 64], vn[half, hd(h)], False, True)
            k_ = PEQ.last()
            po[n, f] = [k_]
            fr["C", f] = [act(oR[half, p, hh_[f]], C_[f][half, :], ACT.Copy, k_)]
        if n % 2 and n < 7:
            jz = read_out(p, G, G)
    jz2 = read_out(3, V, V)
    for b in banks:
        b.free = VEQ.last()
    barrier()
    end = barrier()
    x2 = LD.put(lambda e: e.dma_start(x, x_d.rearrange("(t p) d -> p t d", p=128)), end)
    wread[:] = [list(end), list(end)]
    OT = part(12288), part(16384)
    first = two_parts(first)
    mo = transposed2(oR, OT, jz, jz2)
    j = barrier()
    gr = row_of(gts[1][0], GROW, DIAG)
    out_proj(OT, I["gdn_out_w_2"][0], keep_rows, mo, first)
    two_parts_end()
    xn = tiles(lambda t: square(t, XN[:, t, :], 0, VEQ.last()), post(GROW, gr, x2), again)
    moe2(1, xn, None)

    block = ctx.enter_context(nc.Block())
    ends = AD.marks()

    def emit(q, tailw=()):
        def waits_of(eng, waits, seen):
            need = {}
            for w in waits:
                w = w() if callable(w) else w
                for s, n in (w if isinstance(w, list) else [w]):
                    if n > seen.get(s, 0):
                        need[s] = max(need.get(s, 0), n)
            for s, n in need.items():
                eng.wait_ge(s, n)
                seen[s] = n

        def run(eng, ops, seen):
            for op in ops:
                if op[0] is None:
                    _, over, inner, made = op
                    if not inner:
                        continue
                    with eng.If(over(eng)):
                        run(eng, inner, dict(seen))
                    with eng.Else():
                        for s, before, n in made:
                            if before:
                                eng.wait_ge(s, before)
                            eng.sem_inc(s, n)
                    continue
                fn, waits, inc, _ = op
                waits_of(eng, waits, seen)
                i = fn(eng)
                if inc:
                    i.then_inc(*inc)

        def go(eng):
            run(eng, q.ops, {})
            for s, n in tailw:
                eng.wait_ge(s, n)
        return go

    block.sync(emit(SPQ))
    block.tensor(emit(PEQ))
    block.vector(emit(VEQ))
    block.gpsimd(emit(GPQ))
    block.scalar(emit(ACQ, ends))
    ctx.close()


_INS = ["x", "c", "ctx", "c_ctx", "w_mod", "b_mod", "norm1_g", "norm2_g", "hg_w_in", "hg_lb_fwd", "hg_lb_bwd",
        "hg_gnorm", "hg_w_out", "router_w", "router_b", "moe_w_gate", "moe_w_up", "moe_w_down", "final_g", "c_2",
        "ada_w_2", "ada_b_2", "norm_w_2", "conv_in_w_2", "conv_w_2", "conv_out_w_2", "gdn_in_w_2", "gdn_conv_w_2",
        "gdn_a_log_2", "gdn_dt_bias_2", "gdn_norm_w_2", "gdn_out_w_2", "moe_group_w_2", "moe_group_b_2",
        "moe_expert_w_2", "moe_expert_b_2", "moe_w_gate_2", "moe_w_up_2", "moe_w_down_2", "shared_w_gate_2",
        "shared_w_up_2", "shared_w_down_2", "shared_gate_w_2"]


def kernel(**inputs):
    import numpy as np
    import concourse.bacc as bacc
    from concourse import mybir
    from concourse.bass_utils import run_bass_kernel_spmd

    nc = bacc.Bacc("TRN2", target_bir_lowering=False, num_devices=1)
    arrays, aps = {}, {}
    for name in _INS:
        a = np.ascontiguousarray(inputs[name])
        arrays[f"in_{name}"] = a
        aps[name] = nc.dram_tensor(f"in_{name}", a.shape, mybir.dt.from_np(a.dtype), kind="ExternalInput").ap()
    out = nc.dram_tensor("out_0", (1, NTOK, F), mybir.dt.float32, kind="ExternalOutput").ap()
    program(nc, aps, out)
    r = run_bass_kernel_spmd(nc, [arrays], core_ids=[0])
    return r.results[0]["out_0"]
```
